# Optimizing a Trainium2 kernel written in Bass

```python
import jax, jax.numpy as jnp
from jax import lax
import numpy as np
import math

D_MODEL = 1024
BATCH = 1
SEQ = 512
DEPTH = 2

N_MEM = 256
EPS = 1e-6
SC_WIDTH = D_MODEL // 2
SC_GROUPS = 8
CONV_K = 3
POOL_WIDTH = D_MODEL // 2
POOL_WINDOWS = (2, 4, 8, 16)
POOL_GROUP = POOL_WIDTH // len(POOL_WINDOWS)
EVEN_IN = 3 * SC_WIDTH + POOL_WIDTH
EVEN_MIX = SC_WIDTH + POOL_WIDTH
ML_HEADS = 4
ML_HEAD_DIM = 128
ML_WIDTH = ML_HEADS * ML_HEAD_DIM
ML_CHUNK = 64
MLA_HEADS = 8
QK_NOPE = 64
QK_ROPE = 32
V_DIM = 64
Q_LORA = 384
KV_LORA = 256
MLA_WIDTH = MLA_HEADS * V_DIM
Q_BLOCK = 128
ROPE_THETA = 10000.0
ODD_SIZES = (ML_WIDTH, ML_WIDTH, ML_WIDTH, ML_WIDTH, 2 * ML_HEADS, Q_LORA, KV_LORA, QK_ROPE)
ODD_SPLIT = tuple(int(v) for v in np.cumsum(ODD_SIZES)[:-1])
ODD_IN = sum(ODD_SIZES)
ODD_MIX = ML_WIDTH + MLA_WIDTH
XA_HEADS = 4
XA_HEAD_DIM = 128
XA_WIDTH = XA_HEADS * XA_HEAD_DIM
FFN_HIDDEN = ((8 * D_MODEL + 3 * 256 - 1) // (3 * 256)) * 256
N_EVEN = (DEPTH + 1) // 2
N_ODD = DEPTH // 2


def rmsnorm(x, g):
    xf = x.astype(jnp.float32)
    y = xf * lax.rsqrt(jnp.mean(xf * xf, axis=-1, keepdims=True) + EPS)
    return (y * g.astype(jnp.float32)).astype(x.dtype)

def causal_dwconv(u, w):
    c = u.shape[-1]
    return lax.conv_general_dilated(u, w[:, None, :].astype(u.dtype), window_strides=(1,),
                                    padding=[(CONV_K - 1, 0)],
                                    dimension_numbers=('NWC', 'WIO', 'NWC'),
                                    feature_group_count=c)

def causal_pool_mixer(u, pool_w, pool_scale):
    B, S, _ = u.shape
    ug = u.reshape(B, S, len(POOL_WINDOWS), POOL_GROUP)
    csum = jnp.cumsum(ug.astype(jnp.float32), axis=1)
    t1 = jnp.arange(1, S + 1)
    means = []
    for gi, w in enumerate(POOL_WINDOWS):
        cg = csum[:, :, gi]
        shifted = jnp.pad(cg, ((0, 0), (w, 0), (0, 0)))[:, :S]
        cnt = jnp.minimum(t1, w).astype(jnp.float32)
        means.append((cg - shifted) / cnt[None, :, None])
    pooled = jnp.stack(means, axis=2).astype(u.dtype)
    y = jnp.einsum('bsgc,gcd->bsgd', pooled - ug, pool_w)
    return y.reshape(B, S, POOL_WIDTH) * pool_scale

def even_mixer(h, w_in, conv_w, pool_w, pool_scale, w_out):
    z = h @ w_in
    g_b, g_c, xa, xb = jnp.split(z, [SC_WIDTH, 2 * SC_WIDTH, 3 * SC_WIDTH], axis=-1)
    ya = g_b * causal_dwconv(g_c * xa, conv_w)
    yb = causal_pool_mixer(xb, pool_w, pool_scale)
    return jnp.concatenate([ya, yb], axis=-1) @ w_out

def mlstm_chunkwise(q, k, v, i_pre, f_pre):
    B, S, H, D = q.shape
    L = ML_CHUNK
    NC = S // L

    def chunk(t):
        return t.reshape(B, NC, L, H, D).transpose(0, 3, 1, 2, 4)

    def chunk_g(t):
        return t.reshape(B, NC, L, H).transpose(0, 3, 1, 2)

    qc, kc, vc = chunk(q), chunk(k) * (D ** -0.5), chunk(v)
    ig = chunk_g(i_pre)
    bcum = jnp.cumsum(chunk_g(jax.nn.log_sigmoid(f_pre)), axis=-1)
    gtot = bcum[..., -1]

    a = gtot[..., None] - bcum + ig
    m_loc = jnp.max(a, axis=-1)
    w_loc = jnp.exp(a - m_loc[..., None])
    C_loc = jnp.einsum('bhcl,bhclv,bhclk->bhcvk', w_loc, vc, kc)
    n_loc = jnp.einsum('bhcl,bhclk->bhck', w_loc, kc)

    def step(carry, xs):
        C, n, m = carry
        g_c, m_l, C_l, n_l = xs
        m_new = jnp.maximum(g_c + m, m_l)
        s_old = jnp.exp(g_c + m - m_new)
        s_new = jnp.exp(m_l - m_new)
        C_new = s_old[..., None, None] * C + s_new[..., None, None] * C_l
        n_new = s_old[..., None] * n + s_new[..., None] * n_l
        return (C_new, n_new, m_new), (C, n, m)

    init = (jnp.zeros((B, H, D, D), jnp.float32), jnp.zeros((B, H, D), jnp.float32),
            jnp.zeros((B, H), jnp.float32))
    xs = (jnp.moveaxis(gtot, 2, 0), jnp.moveaxis(m_loc, 2, 0),
          jnp.moveaxis(C_loc, 2, 0), jnp.moveaxis(n_loc, 2, 0))
    _, (C_prev, n_prev, m_prev) = lax.scan(step, init, xs)
    C_prev = jnp.moveaxis(C_prev, 0, 2)
    n_prev = jnp.moveaxis(n_prev, 0, 2)
    m_prev = jnp.moveaxis(m_prev, 0, 2)

    causal = jnp.tril(jnp.ones((L, L), dtype=bool))
    dmat = jnp.where(causal, bcum[..., :, None] - bcum[..., None, :] + ig[..., None, :], -jnp.inf)
    inter = bcum + m_prev[..., None]
    m_t = jnp.maximum(inter, jnp.max(dmat, axis=-1))
    w_intra = jnp.exp(dmat - m_t[..., None])
    w_inter = jnp.exp(inter - m_t)
    sw = w_intra * jnp.einsum('bhcld,bhcsd->bhcls', qc, kc)
    num = (w_inter[..., None] * jnp.einsum('bhcvk,bhclk->bhclv', C_prev, qc)
           + jnp.einsum('bhcls,bhcsv->bhclv', sw, vc))
    den_raw = w_inter * jnp.einsum('bhck,bhclk->bhcl', n_prev, qc) + jnp.sum(sw, axis=-1)
    den = jnp.maximum(jnp.abs(den_raw), jnp.exp(-m_t))
    hc = num / den[..., None]
    return hc.transpose(0, 2, 3, 1, 4).reshape(B, S, H, D)

def rope_tables(positions):
    half = QK_ROPE // 2
    inv_freq = ROPE_THETA ** (-jnp.arange(half, dtype=jnp.float32) / half)
    ang = positions.astype(jnp.float32)[..., None] * inv_freq
    return jnp.cos(ang)[:, :, None, :], jnp.sin(ang)[:, :, None, :]

def apply_rope(t, cos, sin):
    half = t.shape[-1] // 2
    tf = t.astype(jnp.float32)
    t1, t2 = tf[..., :half], tf[..., half:]
    return jnp.concatenate([t1 * cos - t2 * sin, t1 * sin + t2 * cos], axis=-1).astype(t.dtype)

def mla_attention(q_nope, q_rope, k_nope, k_rope, v):
    B, S, H, _ = q_nope.shape
    nb = S // Q_BLOCK
    scale = (QK_NOPE + QK_ROPE) ** -0.5
    k_idx = jnp.arange(S)

    def to_blocks(t):
        return jnp.moveaxis(t.reshape(B, nb, Q_BLOCK, H, t.shape[-1]), 1, 0)

    def attend_block(args):
        blk, qn, qr = args
        s = (jnp.einsum('bqhd,bkhd->bhqk', qn, k_nope)
             + jnp.einsum('bqhr,bkr->bhqk', qr, k_rope)).astype(jnp.float32) * scale
        q_idx = blk * Q_BLOCK + jnp.arange(Q_BLOCK)
        s = jnp.where(k_idx[None, :] <= q_idx[:, None], s, -jnp.inf)
        p = jax.nn.softmax(s, axis=-1).astype(v.dtype)
        return jnp.einsum('bhqk,bkhd->bqhd', p, v)

    out = lax.map(attend_block, (jnp.arange(nb), to_blocks(q_nope), to_blocks(q_rope)))
    return jnp.moveaxis(out, 0, 1).reshape(B, S, H * V_DIM)

def odd_mixer(h, positions, w_in, gate_bias, ml_norm_g, q_norm_g, kv_norm_g, w_uq, w_ukv, w_out):
    B, S, _ = h.shape
    z = h @ w_in
    q_m, k_m, v_m, o_m, gates, c_q, c_kv, k_r = jnp.split(z, ODD_SPLIT, axis=-1)
    gates = (gates + gate_bias).astype(jnp.float32)
    i_pre, f_pre = gates[..., :ML_HEADS], gates[..., ML_HEADS:]
    hs = (B, S, ML_HEADS, ML_HEAD_DIM)
    hm = mlstm_chunkwise(q_m.reshape(hs).astype(jnp.float32), k_m.reshape(hs).astype(jnp.float32),
                         v_m.reshape(hs).astype(jnp.float32), i_pre, f_pre).astype(h.dtype)
    hm = jax.nn.sigmoid(o_m).reshape(hs) * hm
    hm = rmsnorm(hm, ml_norm_g.reshape(ML_HEADS, ML_HEAD_DIM)).reshape(B, S, ML_WIDTH)

    q = (rmsnorm(c_q, q_norm_g) @ w_uq).reshape(B, S, MLA_HEADS, QK_NOPE + QK_ROPE)
    kv = (rmsnorm(c_kv, kv_norm_g) @ w_ukv).reshape(B, S, MLA_HEADS, QK_NOPE + V_DIM)
    cos, sin = rope_tables(positions)
    q_nope, q_rope = q[..., :QK_NOPE], apply_rope(q[..., QK_NOPE:], cos, sin)
    k_nope, v = kv[..., :QK_NOPE], kv[..., QK_NOPE:]
    k_rope = apply_rope(k_r[:, :, None, :], cos, sin)[:, :, 0]
    ha = mla_attention(q_nope, q_rope, k_nope, k_rope, v)
    return jnp.concatenate([hm, ha], axis=-1) @ w_out

def memory_cross_attention(h, mem_n, wq, wkv, wo):
    B, S, _ = h.shape
    q = (h @ wq).reshape(B, S, XA_HEADS, XA_HEAD_DIM)
    k, v = jnp.split(mem_n @ wkv, 2, axis=-1)
    k = k.reshape(B, N_MEM, XA_HEADS, XA_HEAD_DIM)
    v = v.reshape(B, N_MEM, XA_HEADS, XA_HEAD_DIM)
    s = jnp.einsum('bshd,bmhd->bhsm', q, k).astype(jnp.float32) * (XA_HEAD_DIM ** -0.5)
    p = jax.nn.softmax(s, axis=-1).astype(v.dtype)
    return jnp.einsum('bhsm,bmhd->bshd', p, v).reshape(B, S, XA_WIDTH) @ wo

def swiglu(h, w_gate_up, w_down):
    g, u = jnp.split(h @ w_gate_up, 2, axis=-1)
    return (jax.nn.silu(g) * u) @ w_down

def first_inputs(seed: int = 0) -> dict:
    key = jax.random.key(seed)
    ks = iter(jax.random.split(key, 40))
    f32 = jnp.float32

    def dense(shape, fan_in):
        return jax.random.normal(next(ks), shape, f32) * (fan_in ** -0.5)

    def gain(shape):
        return 1.0 + 0.05 * jax.random.normal(next(ks), shape, f32)

    x = jax.random.normal(next(ks), (BATCH, SEQ, D_MODEL), f32)
    mem = jax.random.normal(next(ks), (BATCH, N_MEM, D_MODEL), f32)
    offsets = jax.random.randint(next(ks), (BATCH, 1), 0, 1024, dtype=jnp.int32)
    positions = offsets + jnp.arange(SEQ, dtype=jnp.int32)[None, :]

    f_bias = jnp.linspace(3.0, 6.0, ML_HEADS, dtype=f32)[None, :] + 0.1 * jax.random.normal(next(ks), (N_ODD, ML_HEADS), f32)
    i_bias = 0.1 * jax.random.normal(next(ks), (N_ODD, ML_HEADS), f32)

    return {
        'x': x,
        'mem': mem,
        'positions': positions,
        'norm_mix_g': gain((DEPTH, D_MODEL)),
        'norm_xattn_g': gain((DEPTH, D_MODEL)),
        'mem_norm_g': gain((DEPTH, D_MODEL)),
        'xattn_wq': dense((DEPTH, D_MODEL, XA_WIDTH), D_MODEL),
        'xattn_wkv': dense((DEPTH, D_MODEL, 2 * XA_WIDTH), D_MODEL),
        'xattn_wo': dense((DEPTH, XA_WIDTH, D_MODEL), XA_WIDTH),
        'norm_ffn_g': gain((DEPTH, D_MODEL)),
        'ffn_w_gate_up': dense((DEPTH, D_MODEL, 2 * FFN_HIDDEN), D_MODEL),
        'ffn_w_down': dense((DEPTH, FFN_HIDDEN, D_MODEL), FFN_HIDDEN),
        'ev_w_in': dense((N_EVEN, D_MODEL, EVEN_IN), D_MODEL),
        'ev_conv_w': dense((N_EVEN, CONV_K, SC_WIDTH), CONV_K),
        'ev_pool_w': dense((N_EVEN, len(POOL_WINDOWS), POOL_GROUP, POOL_GROUP), POOL_GROUP),
        'ev_pool_scale': 1.0 + 0.1 * jax.random.normal(next(ks), (N_EVEN, POOL_WIDTH), f32),
        'ev_w_out': dense((N_EVEN, EVEN_MIX, D_MODEL), EVEN_MIX),
        'od_w_in': dense((N_ODD, D_MODEL, ODD_IN), D_MODEL),
        'od_gate_bias': jnp.concatenate([i_bias, f_bias], axis=-1),
        'od_ml_norm_g': gain((N_ODD, ML_WIDTH)),
        'od_q_norm_g': gain((N_ODD, Q_LORA)),
        'od_kv_norm_g': gain((N_ODD, KV_LORA)),
        'od_w_uq': dense((N_ODD, Q_LORA, MLA_HEADS * (QK_NOPE + QK_ROPE)), Q_LORA),
        'od_w_ukv': dense((N_ODD, KV_LORA, MLA_HEADS * (QK_NOPE + V_DIM)), KV_LORA),
        'od_w_out': dense((N_ODD, ODD_MIX, D_MODEL), ODD_MIX),
        'final_norm_g': gain((D_MODEL,)),
    }

def first_block(x, mem, positions, norm_mix_g, norm_xattn_g, mem_norm_g, xattn_wq, xattn_wkv, xattn_wo,
              norm_ffn_g, ffn_w_gate_up, ffn_w_down, ev_w_in, ev_conv_w, ev_pool_w, ev_pool_scale,
              ev_w_out, od_w_in, od_gate_bias, od_ml_norm_g, od_q_norm_g, od_kv_norm_g, od_w_uq,
              od_w_ukv, od_w_out, final_norm_g):
    for layer in range(DEPTH):
        h = rmsnorm(x, norm_mix_g[layer])
        if layer % 2 == 0:
            e = layer // 2
            mix = even_mixer(h, ev_w_in[e], ev_conv_w[e], ev_pool_w[e], ev_pool_scale[e], ev_w_out[e])
        else:
            o = layer // 2
            mix = odd_mixer(h, positions, od_w_in[o], od_gate_bias[o], od_ml_norm_g[o], od_q_norm_g[o],
                            od_kv_norm_g[o], od_w_uq[o], od_w_ukv[o], od_w_out[o])
        x = x + mix
        mem_n = rmsnorm(mem, mem_norm_g[layer])
        x = x + memory_cross_attention(rmsnorm(x, norm_xattn_g[layer]), mem_n,
                                       xattn_wq[layer], xattn_wkv[layer], xattn_wo[layer])
        x = x + swiglu(rmsnorm(x, norm_ffn_g[layer]), ffn_w_gate_up[layer], ffn_w_down[layer])
    return rmsnorm(x, final_norm_g)


D_MIX = D_MODEL
N_DIRS = 2
DN_HEADS = 4
DN_DK = 128
DN_DV = 128
DN_KEY = DN_HEADS * DN_DK
DN_VAL = DN_HEADS * DN_DV
DN_CONV = 5
DN_CHUNK = 64
HY_WIDTH = D_MIX - DN_VAL
HY_ORDER = 2
HY_SHORT = 3
HY_EMB = 33
HY_FILTER_HIDDEN = 64
HY_DIRS = 2
HY_FAST_DECAY_PCT = 0.3
HY_SLOW_DECAY_PCT = 1.5
HY_DECAY_TARGET = 1e-2
D_FF = 2816
RMS_EPS = 1e-6

_O_Q = DN_KEY
_O_K = 2 * DN_KEY
_O_V = _O_K + DN_VAL
_O_Z = _O_V + DN_VAL
_O_B = _O_Z + N_DIRS * DN_HEADS
_O_A = _O_B + N_DIRS * DN_HEADS
D_IN = _O_A + 3 * HY_WIDTH
IN_SPLITS = (_O_Q, _O_K, _O_V, _O_Z, _O_B, _O_A)


def _rmsnorm(x, w):
    xf = x.astype(jnp.float32)
    y = xf * lax.rsqrt(jnp.mean(xf * xf, axis=-1, keepdims=True) + RMS_EPS)
    return (y * w.astype(jnp.float32)).astype(x.dtype)

def _l2norm(t):
    return t * lax.rsqrt(jnp.sum(t * t, axis=-1, keepdims=True) + 1e-6)

def _swiglu(h, w_gate, w_up, w_down):
    return (jax.nn.silu(h @ w_gate) * (h @ w_up)) @ w_down

def _dwconv(x, w):
    k = w.shape[0]
    return lax.conv_general_dilated(
        x, w[:, None, :].astype(x.dtype), window_strides=(1,),
        padding=[(k // 2, k // 2)], dimension_numbers=("NWC", "WIO", "NWC"),
        feature_group_count=x.shape[-1])

def _gated_delta_rule(q, k, v, beta, g):
    b, h, l, dk = q.shape
    dv = v.shape[-1]
    c = DN_CHUNK
    n = l // c
    q = q.reshape(b, h, n, c, dk)
    k = k.reshape(b, h, n, c, dk)
    v = v.reshape(b, h, n, c, dv)
    beta = beta.reshape(b, h, n, c)
    g = jnp.cumsum(g.reshape(b, h, n, c), axis=-1)
    incl = jnp.tril(jnp.ones((c, c), bool))
    strict = jnp.tril(jnp.ones((c, c), bool), -1)
    diff = g[..., :, None] - g[..., None, :]
    decay = jnp.where(incl, jnp.exp(jnp.where(incl, diff, 0.0)), 0.0)
    kb = k * beta[..., None]
    a_mat = jnp.where(strict, jnp.einsum("bhnid,bhnjd->bhnij", kb, k) * decay, 0.0)
    a_mat = a_mat + jnp.eye(c, dtype=q.dtype)
    rhs = jnp.concatenate([v * beta[..., None], kb * jnp.exp(g)[..., None]], axis=-1)
    sol = lax.linalg.triangular_solve(a_mat, rhs, left_side=True, lower=True,
                                      unit_diagonal=True)
    u, w = sol[..., :dv], sol[..., dv:]
    attn = jnp.einsum("bhnid,bhnjd->bhnij", q, k) * decay
    g_last = g[..., -1]
    q_dec = q * jnp.exp(g)[..., None]
    k_dec = k * jnp.exp(g_last[..., None] - g)[..., None]

    def step(state, inp):
        q_i, k_i, u_i, w_i, attn_i, gl_i = inp
        v_new = u_i - jnp.einsum("bhcd,bhde->bhce", w_i, state)
        o_i = (jnp.einsum("bhcd,bhde->bhce", q_i, state)
               + jnp.einsum("bhcs,bhse->bhce", attn_i, v_new))
        state = (state * jnp.exp(gl_i)[..., None, None]
                 + jnp.einsum("bhcd,bhce->bhde", k_i, v_new))
        return state, o_i

    xs = tuple(jnp.moveaxis(t, 2, 0) for t in (q_dec, k_dec, u, w, attn, g_last))
    state0 = jnp.zeros((b, h, dk, dv), q.dtype)
    _, o = lax.scan(step, state0, xs)
    return jnp.moveaxis(o, 0, 2).reshape(b, h, l, dv)

def _deltanet_group(q, k, v, z, beta_logit, alpha, a_log, dt_bias, conv_w, norm_w):
    f32 = jnp.float32
    b, l, _ = q.shape
    qkv = jax.nn.silu(_dwconv(jnp.concatenate([q, k, v], axis=-1), conv_w))
    q, k, v = jnp.split(qkv, [DN_KEY, 2 * DN_KEY], axis=-1)

    def to_heads(t, d):
        return t.reshape(b, l, DN_HEADS, d).transpose(0, 2, 1, 3).astype(f32)

    q = _l2norm(to_heads(q, DN_DK)) * (DN_DK ** -0.5)
    k = _l2norm(to_heads(k, DN_DK))
    v = to_heads(v, DN_DV)
    beta = jax.nn.sigmoid(beta_logit.astype(f32)).reshape(b, l, N_DIRS, DN_HEADS).transpose(2, 0, 3, 1)
    a_in = alpha.astype(f32).reshape(b, l, N_DIRS, DN_HEADS).transpose(2, 0, 3, 1)
    g = -jnp.exp(a_log.astype(f32))[:, None, :, None] * jax.nn.softplus(
        a_in + dt_bias.astype(f32)[:, None, :, None])
    o_fwd = _gated_delta_rule(q, k, v, beta[0], g[0])
    flip = lambda t: jnp.flip(t, axis=2)
    o_bwd = flip(_gated_delta_rule(flip(q), flip(k), flip(v), flip(beta[1]), flip(g[1])))
    o = (o_fwd + o_bwd).transpose(0, 2, 1, 3)
    o = _rmsnorm(o, norm_w) * jax.nn.silu(z.reshape(b, l, DN_HEADS, DN_DV).astype(f32))
    return o.reshape(b, l, DN_VAL).astype(z.dtype)

def _hyena_filter_spectrum(l, w1, b1, w2, b2, w3, b3, freq, wout):
    f32 = jnp.float32
    t = jnp.linspace(0.0, 1.0, l, dtype=f32)[:, None]
    bands = (HY_EMB - 1) // 2
    ang = ((2.0 * math.pi / l) * jnp.arange(l, dtype=f32)[:, None]
           * jnp.linspace(1e-4, bands - 1, bands, dtype=f32)[None, :])
    feats = jnp.concatenate([t, jnp.cos(ang), -jnp.sin(ang)], axis=-1)
    fr = freq.astype(f32)
    hdn = jnp.sin(fr * (feats @ w1.astype(f32) + b1.astype(f32)))
    hdn = jnp.sin(fr * (hdn @ w2.astype(f32) + b2.astype(f32)))
    hdn = jnp.sin(fr * (hdn @ w3.astype(f32) + b3.astype(f32)))
    filt = (hdn @ wout.astype(f32)).reshape(l, HY_DIRS, HY_ORDER, HY_WIDTH)
    max_decay = math.log(HY_DECAY_TARGET) / HY_FAST_DECAY_PCT
    min_decay = math.log(HY_DECAY_TARGET) / HY_SLOW_DECAY_PCT
    deltas = jnp.abs(jnp.linspace(min_decay, max_decay, HY_WIDTH, dtype=f32))
    filt = filt * jnp.exp(-t * deltas)[:, None, None, :]
    fwd, bwd = filt[:, 0], filt[:, 1]
    two_sided = jnp.concatenate(
        [fwd, jnp.zeros((1, HY_ORDER, HY_WIDTH), f32), jnp.flip(bwd[: l - 1], axis=0)], axis=0)
    return jnp.fft.rfft(two_sided, axis=0)

def _fft_conv(z, kspec):
    l = z.shape[1]
    zs = jnp.fft.rfft(z, n=2 * l, axis=1)
    return jnp.fft.irfft(zs * kspec[None], n=2 * l, axis=1)[:, :l]

def _hyena_group(u, conv_w, conv_b, w1, b1, w2, b2, w3, b3, freq, wout, skip, norm_w):
    f32 = jnp.float32
    l = u.shape[1]
    u = _dwconv(u, conv_w) + conv_b
    v, x1, x2 = [t.astype(f32) for t in jnp.split(u, 3, axis=-1)]
    kspec = _hyena_filter_spectrum(l, w1, b1, w2, b2, w3, b3, freq, wout)
    skip = skip.astype(f32)
    zz = v
    for o, gate in enumerate((x1, x2)):
        zz = gate * (_fft_conv(zz, kspec[:, o]) + skip[o] * zz)
    return _rmsnorm(zz, norm_w).astype(u.dtype)

def second_inputs(seed: int = 0) -> dict:
    key = jax.random.key(seed)
    ks = iter(jax.random.split(key, 40))
    f32 = jnp.float32

    def nrm(shape, scale):
        return scale * jax.random.normal(next(ks), shape, f32)

    def gain(shape):
        return 1.0 + 0.02 * jax.random.normal(next(ks), shape, f32)

    x = jax.random.normal(next(ks), (BATCH, SEQ, D_MODEL), f32)
    a_log = jnp.log(jax.random.uniform(next(ks), (DEPTH, N_DIRS, DN_HEADS), f32, 1.0, 16.0))
    dt = jnp.exp(jax.random.uniform(next(ks), (DEPTH, N_DIRS, DN_HEADS), f32,
                                    math.log(1e-3), math.log(1e-1)))
    dt_bias = dt + jnp.log(-jnp.expm1(-dt))
    hf = HY_FILTER_HIDDEN
    return {
        "x": x,
        "ffn1_norm": gain((DEPTH, D_MODEL)),
        "ffn1_w_gate": nrm((DEPTH, D_MODEL, D_FF), D_MODEL ** -0.5),
        "ffn1_w_up": nrm((DEPTH, D_MODEL, D_FF), D_MODEL ** -0.5),
        "ffn1_w_down": nrm((DEPTH, D_FF, D_MODEL), D_FF ** -0.5),
        "mix_norm": gain((DEPTH, D_MODEL)),
        "w_in": nrm((DEPTH, D_MODEL, D_IN), D_MODEL ** -0.5),
        "dn_conv": nrm((DEPTH, DN_CONV, 2 * DN_KEY + DN_VAL), DN_CONV ** -0.5),
        "dn_a_log": a_log,
        "dn_dt_bias": dt_bias,
        "dn_norm": gain((DEPTH, DN_DV)),
        "hy_conv": nrm((DEPTH, HY_SHORT, 3 * HY_WIDTH), HY_SHORT ** -0.5),
        "hy_conv_bias": nrm((DEPTH, 3 * HY_WIDTH), 0.02),
        "hy_f_w1": nrm((DEPTH, HY_EMB, hf), HY_EMB ** -0.5),
        "hy_f_b1": nrm((DEPTH, hf), 0.1),
        "hy_f_w2": nrm((DEPTH, hf, hf), hf ** -0.5),
        "hy_f_b2": nrm((DEPTH, hf), 0.1),
        "hy_f_w3": nrm((DEPTH, hf, hf), hf ** -0.5),
        "hy_f_b3": nrm((DEPTH, hf), 0.1),
        "hy_f_freq": gain((DEPTH, hf)),
        "hy_f_wout": nrm((DEPTH, hf, HY_DIRS * HY_ORDER * HY_WIDTH), 0.05 * hf ** -0.5),
        "hy_skip": nrm((DEPTH, HY_ORDER, HY_WIDTH), 1.0),
        "hy_norm": gain((DEPTH, HY_WIDTH)),
        "w_out": nrm((DEPTH, D_MIX, D_MODEL), D_MIX ** -0.5),
        "ffn2_norm": gain((DEPTH, D_MODEL)),
        "ffn2_w_gate": nrm((DEPTH, D_MODEL, D_FF), D_MODEL ** -0.5),
        "ffn2_w_up": nrm((DEPTH, D_MODEL, D_FF), D_MODEL ** -0.5),
        "ffn2_w_down": nrm((DEPTH, D_FF, D_MODEL), D_FF ** -0.5),
        "final_norm": gain((D_MODEL,)),
    }

def second_block(x, ffn1_norm, ffn1_w_gate, ffn1_w_up, ffn1_w_down, mix_norm, w_in,
              dn_conv, dn_a_log, dn_dt_bias, dn_norm, hy_conv, hy_conv_bias,
              hy_f_w1, hy_f_b1, hy_f_w2, hy_f_b2, hy_f_w3, hy_f_b3, hy_f_freq,
              hy_f_wout, hy_skip, hy_norm, w_out, ffn2_norm, ffn2_w_gate,
              ffn2_w_up, ffn2_w_down, final_norm):
    for i in range(DEPTH):
        x = x + 0.5 * _swiglu(_rmsnorm(x, ffn1_norm[i]), ffn1_w_gate[i], ffn1_w_up[i], ffn1_w_down[i])
        proj = _rmsnorm(x, mix_norm[i]) @ w_in[i]
        q, k, v, z, beta_logit, alpha, hy_in = jnp.split(proj, IN_SPLITS, axis=-1)
        o_dn = _deltanet_group(q, k, v, z, beta_logit, alpha, dn_a_log[i], dn_dt_bias[i],
                               dn_conv[i], dn_norm[i])
        o_hy = _hyena_group(hy_in, hy_conv[i], hy_conv_bias[i], hy_f_w1[i], hy_f_b1[i],
                            hy_f_w2[i], hy_f_b2[i], hy_f_w3[i], hy_f_b3[i], hy_f_freq[i],
                            hy_f_wout[i], hy_skip[i], hy_norm[i])
        x = x + jnp.concatenate([o_dn, o_hy], axis=-1) @ w_out[i]
        x = x + 0.5 * _swiglu(_rmsnorm(x, ffn2_norm[i]), ffn2_w_gate[i], ffn2_w_up[i], ffn2_w_down[i])
    return _rmsnorm(x, final_norm)


def setup_inputs(seed=0):
    out = dict(first_inputs(seed))
    for name, value in second_inputs(seed + 1).items():
        if name != "x":
            out[name + "_2"] = value
    return out


def reference(
    x, mem, positions, norm_mix_g, norm_xattn_g, mem_norm_g, xattn_wq, xattn_wkv, xattn_wo,
    norm_ffn_g, ffn_w_gate_up, ffn_w_down, ev_w_in, ev_conv_w, ev_pool_w, ev_pool_scale,
    ev_w_out, od_w_in, od_gate_bias, od_ml_norm_g, od_q_norm_g, od_kv_norm_g, od_w_uq, od_w_ukv,
    od_w_out, final_norm_g, ffn1_norm_2, ffn1_w_gate_2, ffn1_w_up_2, ffn1_w_down_2, mix_norm_2,
    w_in_2, dn_conv_2, dn_a_log_2, dn_dt_bias_2, dn_norm_2, hy_conv_2, hy_conv_bias_2,
    hy_f_w1_2, hy_f_b1_2, hy_f_w2_2, hy_f_b2_2, hy_f_w3_2, hy_f_b3_2, hy_f_freq_2, hy_f_wout_2,
    hy_skip_2, hy_norm_2, w_out_2, ffn2_norm_2, ffn2_w_gate_2, ffn2_w_up_2, ffn2_w_down_2,
    final_norm_2,
):
    x = first_block(
        x, mem, positions, norm_mix_g, norm_xattn_g, mem_norm_g, xattn_wq, xattn_wkv, xattn_wo,
        norm_ffn_g, ffn_w_gate_up, ffn_w_down, ev_w_in, ev_conv_w, ev_pool_w, ev_pool_scale,
        ev_w_out, od_w_in, od_gate_bias, od_ml_norm_g, od_q_norm_g, od_kv_norm_g, od_w_uq,
        od_w_ukv, od_w_out, final_norm_g,
    )
    return second_block(
        x, ffn1_norm_2, ffn1_w_gate_2, ffn1_w_up_2, ffn1_w_down_2, mix_norm_2, w_in_2,
        dn_conv_2, dn_a_log_2, dn_dt_bias_2, dn_norm_2, hy_conv_2, hy_conv_bias_2, hy_f_w1_2,
        hy_f_b1_2, hy_f_w2_2, hy_f_b2_2, hy_f_w3_2, hy_f_b3_2, hy_f_freq_2, hy_f_wout_2,
        hy_skip_2, hy_norm_2, w_out_2, ffn2_norm_2, ffn2_w_gate_2, ffn2_w_up_2, ffn2_w_down_2,
        final_norm_2,
    )


_drawn_inputs = setup_inputs


def setup_inputs(seed=0):
    import zlib

    import numpy as np

    out = dict(_drawn_inputs(seed))
    spreads = {}
    factors = {'norm_xattn_g': 4.639,
     'mem_norm_g': 3.179,
     'od_q_norm_g': 8.0,
     'od_kv_norm_g': 6.548,
     'ffn1_norm_2': 3.444,
     'dn_norm_2': 19.439,
     'hy_f_freq_2': 8.0,
     'hy_norm_2': 13.217,
     'ffn2_norm_2': 5.882,
     'final_norm_2': 8.42}
    for name, (base, spread) in spreads.items():
        noise = np.random.default_rng([zlib.crc32(name.encode()), seed]).standard_normal(out[name].shape)
        drawn = base * np.exp(spread * noise) if base else spread * noise
        out[name] = __import__('jax').numpy.asarray(drawn.astype(out[name].dtype))
    for name, factor in factors.items():
        out[name] = (out[name] * factor).astype(out[name].dtype)
    return out
```

```python
from contextlib import ExitStack

import numpy as np

import concourse.bass as bass
from concourse import mybir

ALU = mybir.AluOpType
ACT = mybir.ActivationFunctionType
AX = mybir.AxisListType
F32 = mybir.dt.float32
F32R = mybir.dt.float32r

P = 128
S = 512
TC = S // P
D = 1024
KD = D // P
M_MEM = 256
MC = M_MEM // P
FF = 2816
KF = FF // P
TILES = 16
EPS = 1e-6
XH = 4
NEG = -1e30
TURN = float(np.float32(1 / (2 * np.pi)))
ROUND = 12582912.0
PI2 = (6.28125, 4059 / 2 ** 21, float(2 * np.pi - 6.28125 - 4059 / 2 ** 21))
PI_IN = 3.1415925


class Stage:

    def __init__(self, kind, name="", gain="", src="", dest="", out="", chunks=0, n=0, c0=0, d0=0, k0=0,
                 nb=0, kc=0, upb=1, bpu=1, scale=1.0, layer=0, step=0, half=False, whole=False):
        self.kind, self.name = kind, name
        self.gain = gain
        self.src, self.c0 = src, c0
        self.dest, self.d0 = dest, d0
        self.out, self.scale = out, scale
        self.chunks = chunks
        self.n = n or chunks
        self.k0 = k0
        self.nb, self.kc, self.upb, self.bpu = nb, kc, upb, bpu
        self.layer, self.step = layer, step
        self.half = half
        self.whole = whole
        self.feeds = None
        self.late = False


def linear(name, nblocks, kc, upb=1, bpu=1, out="fm", **kw):
    return Stage("linear", name=name, nb=nblocks, kc=kc, upb=upb, bpu=bpu, out=out, chunks=0, **kw)


def ffn(name, norm, scale):
    return [Stage("norm", gain=norm, src="X", c0=0, d0=0, chunks=KD),
            linear(name + "_gu", KF, KD, out="ffn"),
            linear(name + "_down", D // 256, KF, upb=3, out="resid", scale=scale, src="hid")]


def cross_attention(layer):
    return [Stage("mem", gain=f"mem{layer}", chunks=KD),
            linear(f"xk{layer}", 2, KD, out="fm_mem"),
            linear(f"xv{layer}", 2, KD, out="tm_mem"),
            Stage("norm", gain=f"xattn{layer}", src="X", c0=0, d0=0, chunks=KD),
            linear(f"xq{layer}", 2, KD, out="fm", dest="XQ"),
            Stage("xattn", chunks=XH),
            linear(f"xo{layer}", 4, 4, bpu=2, out="resid", scale=1.0, src="h")]


def schedule():
    stages = []
    stages += [Stage("norm", gain="mix0", src="X", c0=0, d0=0, chunks=KD), linear("ev_in", 8, KD, out="even"),
               Stage("even", chunks=8), linear("ev_out", 4, KD, out="resid", scale=1.0, src="h")]
    stages += cross_attention(0) + ffn("ffn0", "ffn0", 1.0)
    stages += [Stage("norm", gain="mix1", src="X", c0=0, d0=0, chunks=KD),
               linear("od_v", 2, KD, out="tm", dest="MV"), Stage("rope", chunks=0), linear("od_in", 9, KD, out="fm", dest="OZ"),
               Stage("norm", gain="qn", src="Z", c0=12, d0=0, chunks=3),
               Stage("norm", gain="kvn", src="Z", c0=15, d0=3, chunks=2),
               linear("uq_nope", 2, 3, out="nope", dest="QM", whole=True), linear("uq_rope", 1, 3, out="fm", dest="QR", whole=True),
               linear("kv_nope", 2, 2, out="nope", dest="KM", k0=3, whole=True), linear("kv_v", 2, 2, out="tm", dest="VM", k0=3, whole=True),
               Stage("mla", chunks=4), Stage("mlstm", chunks=4),
               linear("od_out", 4, KD, out="resid", scale=1.0, src="h", whole=True)]
    stages += cross_attention(1) + ffn("ffn1", "ffn1", 1.0)
    stages += [Stage("rms", gain="final", src="X", c0=0, chunks=0, n=KD)]
    for l in range(2):
        stages += ffn(f"b{l}f1", f"ffn1n{l}", 0.5)
        stages += [Stage("norm", gain=f"mixn{l}", src="X", c0=0, d0=0, chunks=KD),
                   linear(f"b{l}qkv", 6, KD, out="conv5", dest="DQ", layer=l), Stage("net", step=0, layer=l),
                   linear(f"b{l}zg", 3, KD, out="fm", dest="DZ", half=True),
                   Stage("silu_qk", chunks=0), Stage("net", step=1, layer=l),
                   linear(f"b{l}hy", 6, KD, out="conv3", dest="HY", layer=l), Stage("net", step=2, layer=l),
                   Stage("delta", chunks=4, layer=l), Stage("hyena", chunks=0, layer=l),
                   Stage("norm", gain=f"hyn{l}", src="HY", c0=0, d0=4, chunks=4),
                   linear(f"b{l}out", 4, KD, out="resid", scale=1.0, src="h", whole=True)]
        stages += ffn(f"b{l}f2", f"ffn2n{l}", 0.5)
    stages += [Stage("rms", gain="final2", src="X", c0=0, chunks=0, n=KD)]
    u = b = h = norms = ffns = squares = 0
    seen = {}
    prev = None
    plain = 0
    for st in stages:
        st.plain = plain
        st.late = st.kind == "norm" and st.src == "X"
        st.own, st.early = st.n, 0
        if st.kind in ("norm", "rms"):
            plain += not st.late
            if st.src == "X" and prev is not None and prev.out == "resid":
                prev.feeds, st.own = st, 2
                if prev.src == "hid" and st.late:
                    st.early = st.n - 2
        st.opens = st.kind == "linear" and prev is not None and prev.late
        if st.kind == "linear":
            st.scaled = st.out != "resid" and (st.opens or (prev.kind in ("linear", "silu_qk", "rope", "net") and scaled))
            st.norm = prev if st.opens else None
            scaled = st.scaled
        elif st.kind not in ("silu_qk", "rope", "net"):
            scaled = False
        prev = st
        st.u0, st.b0, st.h0, st.nrm, st.ffn, st.sq0 = u, b, h, norms, ffns, squares
        st.nth = seen.get(st.kind, 0)
        seen[st.kind] = st.nth + 1
        if st.kind == "linear":
            st.nu = st.nb * st.upb // st.bpu
            key = "linear:" + st.out
            st.nth_out = seen.get(key, 0)
            seen[key] = st.nth_out + 1
            st.hin = hin
            st.hall = h
            u += st.nu
            b += st.nb
            st.hidin = KF * (ffns - 1)
            ffns += st.out == "ffn"
        else:
            if st.chunks:
                hin = h
            h += st.chunks
            if st.kind in ("norm", "rms"):
                norms += 1
                squares += st.n
    hyenas = [st for st in stages if st.kind == "norm" and st.src == "HY"]
    for n, st in enumerate(hyenas):
        st.nrm_hy = n
    for st in stages:
        st.n_blocks = b
        st.last = st.kind == "linear" and st.u0 + st.nu == u
    return stages, u


def unit_fm(w, cols, ks):
    part = w[:, cols].reshape(-1, P, len(cols))[ks]
    part = part.transpose(1, 0, 2).reshape(P, -1)
    return np.pad(part, ((0, 0), (0, TILES * P - part.shape[1])))


def units_plain(w, kc=None):
    kc = w.shape[0] // P
    return [unit_fm(w, np.arange(c, min(c + 256, w.shape[1])), slice(k, k + 8))
            for c in range(0, w.shape[1], 256) for k in range(0, kc, 8)]


def units_pairs(w, firsts, seconds):
    return [unit_fm(w, np.concatenate([np.arange(a, a + P), np.arange(b, b + P)]), slice(0, 8))
            for a, b in zip(firsts, seconds)]


def units_half(w):
    out = []
    for c in range(0, w.shape[1], 512):
        a = [w[:, c + o:c + o + 256].reshape(4, P, 256).transpose(1, 0, 2).reshape(P, -1) for o in (0, 256)]
        out.append(np.concatenate(a, 1))
    return out


def pack_weights(t, stages):
    even = [c * P for c in range(4)]
    units = []
    for st in stages:
        if st.kind != "linear":
            continue
        n = st.name
        l = int(n.split("_")[0][-1]) if n.split("_")[0][-1].isdigit() else 0
        if n == "ev_in":
            w = t["ev_w_in"][0]
            new = []
            for c in even:
                new += units_pairs(w, [512 + c, c], [1024 + c, 1536 + c])
        elif n == "ev_out":
            new = units_plain(t["ev_w_out"][0])
        elif n[0] == "b":
            l = int(n[1])
            w = t["w_in_2"][l]
            if n[2:] == "qkv":
                new = units_plain(w[:, 0:1536])
            elif n[2:] == "zg":
                new = units_plain(np.concatenate([w[:, 1536:2064], np.zeros((D, 240), np.float32)], 1))
            elif n[2:] == "hy":
                new = units_plain(w[:, 2064:3600])
            elif n[2:] == "out":
                new = units_plain(t["w_out_2"][l])
            elif n.endswith("gu"):
                f = n[3]
                new = units_pairs(np.concatenate([t[f"ffn{f}_w_gate_2"][l], t[f"ffn{f}_w_up_2"][l]], 1),
                                  range(0, FF, P), range(FF, 2 * FF, P))
            else:
                new = units_plain(t[f"ffn{n[3]}_w_down_2"][l])
        elif n == "od_v":
            new = units_plain(t["od_w_in"][0][:, 1024:1536])
        elif n == "od_in":
            w = t["od_w_in"][0]
            kr, gates = w[:, 2696:2728], w[:, 2048:2056]
            new = units_plain(np.concatenate([w[:, 0:1024], w[:, 1536:2048], w[:, 2056:2696], kr, gates,
                                              np.zeros((D, P - 40), np.float32)], 1))
        elif n == "uq_nope":
            new = units_plain(t["od_w_uq"][0].reshape(384, 8, 96)[:, :, :64].reshape(384, 512))
        elif n == "uq_rope":
            new = units_plain(t["od_w_uq"][0].reshape(384, 8, 96)[:, :, 64:].reshape(384, 256))
        elif n == "kv_nope":
            new = units_plain(t["od_w_ukv"][0].reshape(256, 8, 128)[:, :, :64].reshape(256, 512))
        elif n == "kv_v":
            new = units_plain(t["od_w_ukv"][0].reshape(256, 8, 128)[:, :, 64:].reshape(256, 512))
        elif n == "od_out":
            new = units_plain(t["od_w_out"][0])
        elif n[:2] == "xk":
            new = units_plain(t["xattn_wkv"][l][:, :512])
        elif n[:2] == "xv":
            new = units_plain(t["xattn_wkv"][l][:, 512:])
        elif n[:2] == "xq":
            new = units_plain(t["xattn_wq"][l])
        elif n[:2] == "xo":
            new = units_half(t["xattn_wo"][l])
        elif n[:3] == "ffn" and n.endswith("_gu"):
            new = units_pairs(t["ffn_w_gate_up"][l], range(0, FF, P), range(FF, 2 * FF, P))
        elif n[:3] == "ffn":
            new = units_plain(t["ffn_w_down"][l])
        assert len(new) == st.nu, (n, len(new), st.nu)
        units += new
    return np.stack(units)


def cols_of(v):
    return np.ascontiguousarray(v.reshape(-1, P).T)


def param_columns():
    names = [("mix0", 8), ("mix1", 8), ("xattn0", 8), ("xattn1", 8), ("mem0", 8), ("mem1", 8),
             ("ffn0", 8), ("ffn1", 8), ("final", 8), ("ev_conv", 12), ("pool_scale", 4),
             ("qn", 3), ("kvn", 2), ("mln", 4), ("gbias", 8)]
    at, out = 0, {}
    for n, w in names:
        out[n] = (at, w)
        at += w
    return out, at


def pack_params(t):
    conv = t["ev_conv_w"][0]
    vals = {"mix0": cols_of(t["norm_mix_g"][0]), "mix1": cols_of(t["norm_mix_g"][1]),
            "xattn0": cols_of(t["norm_xattn_g"][0]), "xattn1": cols_of(t["norm_xattn_g"][1]),
            "mem0": cols_of(t["mem_norm_g"][0]), "mem1": cols_of(t["mem_norm_g"][1]),
            "ffn0": cols_of(t["norm_ffn_g"][0]), "ffn1": cols_of(t["norm_ffn_g"][1]),
            "final": cols_of(t["final_norm_g"]),
            "ev_conv": np.concatenate([cols_of(conv[j]) for j in range(3)], 1),
            "pool_scale": cols_of(t["ev_pool_scale"][0]),
            "qn": cols_of(t["od_q_norm_g"][0]), "kvn": cols_of(t["od_kv_norm_g"][0]),
            "mln": cols_of(t["od_ml_norm_g"][0]),
            "gbias": np.broadcast_to(t["od_gate_bias"][0], (P, 8))}
    where, n = param_columns()
    return np.concatenate([vals[k] for k in where], 1)


def param2_columns():
    out, at = {}, 0
    for l in range(2):
        for n, w in (("ffn1n", 8), ("mixn", 8), ("ffn2n", 8), ("conv5", 60), ("dnn", 1), ("alog", 8), ("dtb", 8),
                     ("conv3", 36), ("conv3b", 12), ("hyn", 4), ("skip", 8), ("mlp", 4)):
            out[f"{n}{l}"] = (at, w)
            at += w
    out["final2"] = (at, 8)
    return out, at + 8


def pack_params2(t):
    vals = {"final2": cols_of(t["final_norm_2"])}
    for l in range(2):
        c5, c3 = t["dn_conv_2"][l], t["hy_conv_2"][l]
        rows64 = np.stack([t["hy_f_b1_2"][l], t["hy_f_b2_2"][l], t["hy_f_b3_2"][l], t["hy_f_freq_2"][l]], 1)
        vals.update({
            f"ffn1n{l}": cols_of(t["ffn1_norm_2"][l]), f"mixn{l}": cols_of(t["mix_norm_2"][l]),
            f"ffn2n{l}": cols_of(t["ffn2_norm_2"][l]),
            f"conv5{l}": np.concatenate([cols_of(c5[j]) for j in range(5)], 1),
            f"dnn{l}": cols_of(t["dn_norm_2"][l]),
            f"alog{l}": np.broadcast_to(t["dn_a_log_2"][l].reshape(-1), (P, 8)),
            f"dtb{l}": np.broadcast_to(t["dn_dt_bias_2"][l].reshape(-1), (P, 8)),
            f"conv3{l}": np.concatenate([cols_of(c3[j]) for j in range(3)], 1),
            f"conv3b{l}": cols_of(t["hy_conv_bias_2"][l]),
            f"hyn{l}": cols_of(t["hy_norm_2"][l]),
            f"skip{l}": np.concatenate([cols_of(t["hy_skip_2"][l][o]) for o in range(2)], 1),
            f"mlp{l}": np.pad(rows64, ((0, 64), (0, 0)))})
    where, _ = param2_columns()
    return np.concatenate([vals[k] for k in where], 1)


def const2_columns():
    i = np.arange(P)
    levels = [(i[:, None] // (2 * b) == i[None, :] // (2 * b)) & (i[:, None] // b != i[None, :] // b)
              for b in (1, 2, 4, 8, 16, 32, 64)]
    parts = {"levels": np.concatenate(levels, 1), "triT": i[:, None] >= i[None, :]}
    at, where = 0, {}
    for k, v in parts.items():
        where[k] = (at, v.shape[1])
        at += v.shape[1]
    return where, np.concatenate(list(parts.values()), 1).astype(np.float32)


def hyena_constants():
    f32 = np.float32
    t = np.linspace(0.0, 1.0, S, dtype=f32)[:, None]
    bands = 16
    ang = (f32(2.0 * np.pi / S) * np.arange(S, dtype=f32)[:, None]) * np.linspace(1e-4, bands - 1, bands, dtype=f32)[None]
    ang = ang.astype(np.float64)
    feats = np.concatenate([t, np.cos(ang), -np.sin(ang)], 1).astype(f32)
    slow, fast = np.log(1e-2) / 1.5, np.log(1e-2) / 0.3
    deltas = np.abs(np.linspace(slow, fast, 512, dtype=f32))
    plain = np.exp(-t.astype(np.float64) * deltas)
    late = np.concatenate([np.zeros((1, 512)), plain[:-1]])
    dec = np.stack([plain, late], 1).reshape(2, P, 2, 2, 512)
    dec = dec.transpose(1, 2, 0, 3, 4).reshape(P, 4, 2, 512)
    w = 2 * np.pi * (np.arange(256) + 0.5) / 1024
    times = np.arange(S).reshape(2, P, 2).transpose(1, 2, 0)
    a = times[..., None] * w
    fwd = np.stack([np.cos(a), np.sin(a)], 1)
    tt = np.arange(S).reshape(256, 2).T
    b = w.reshape(2, P).T[:, None, :, None] * tt[None, :, None, :]
    inv = np.stack([np.cos(b), np.sin(b)], 1) / 512
    mats = np.concatenate([fwd.reshape(P, -1), inv.reshape(P, -1)], 1)
    return feats.T.astype(f32).copy(), dec.astype(f32), mats.astype(f32)


def pack_filters(t):
    return np.stack([np.concatenate([np.pad(t["hy_f_w1_2"][l], ((0, 31), (0, 0))), t["hy_f_w2_2"][l],
                                     t["hy_f_w3_2"][l], t["hy_f_wout_2"][l]], 1) for l in range(2)])



def const_columns():
    ident = np.eye(P, dtype=np.float32)
    invcnt = np.zeros((P, 4, 16), np.float32)
    for g, w in enumerate((2, 4, 8, 16)):
        invcnt[:, g] = 1.0 / np.minimum(np.arange(1, 17), w)
    idx = np.arange(P)
    mask = np.where(idx[None, :] > idx[:, None], NEG, 0.0)
    tri = (idx[:, None] <= idx[None, :]).astype(np.float32)
    rot = np.zeros((P, P), np.float32)
    for p in range(P):
        if p % 32 < 16:
            rot[p + 16, p] = -1.0
        else:
            rot[p - 16, p] = 1.0
    half = 16
    freq = (np.float32(10000.0) ** (-np.arange(half, dtype=np.float32) / np.float32(half))).astype(np.float32)
    parts = {"ident": ident, "invcnt": invcnt.reshape(P, -1), "mask": mask, "tri": tri, "rot": rot, "freq": freq[idx % half][:, None]}
    at, where = 0, {}
    for k, v in parts.items():
        where[k] = (at, v.shape[1])
        at += v.shape[1]
    return where, np.concatenate(list(parts.values()), 1).astype(np.float32)


def build(nc, wall, xT, memT, params, consts, pos, poolw, params2, consts2, feats, decays, mats, filters, out):
    stages, n_units = schedule()
    pcol, n_par = param_columns()
    ccol, cvals = const_columns()
    n_const = cvals.shape[1]
    n_blocks = sum(st.nb for st in stages if st.kind == "linear")

    ctx = ExitStack()
    with ctx:
        top = [(nc.sbuf_base + 31) // 32 * 32]

        def place(name, shape, dt=F32, at=None):
            size = 4 * int(np.prod(shape[1:]))
            size = (size + 31) // 32 * 32
            where = top[0] if at is None else at
            if at is None:
                top[0] += size
            assert where + size <= nc.sbuf_usable_end, (name, where + size, nc.sbuf_usable_end)
            return nc.alloc_sbuf_tensor_at(name, shape, dt, offset=where)

        def arena(start):
            at = [start]

            def put(name, shape, dt=F32):
                t = place(name, shape, dt, at=at[0])
                at[0] += (4 * int(np.prod(shape[1:])) + 31) // 32 * 32
                return t
            put.at = at
            return put

        def sem(name):
            return ctx.enter_context(nc.semaphore(name))

        X = place("X", [P, KD, S])
        hh_at = top[0]
        HH = place("HH", [P, KD, S], F32R)
        hl_at = top[0]
        HL = place("HL", [P, KD, S], F32R)
        RAW = [place(f"RAW{i}", [P, TILES * P]) for i in range(2)]
        WH = [place(f"WH{i}", [P, TILES * P], F32R) for i in range(2)]
        WL = [place(f"WL{i}", [P, TILES * P], F32R) for i in range(2)]
        mem_at = top[0]
        MEM = place("MEM", [P, KD, M_MEM])
        PAR = place("PAR", [P, n_par])
        CON = place("CON", [P, n_const])
        ONES = place("ONES", [P, P])
        EPSC = place("EPSC", [P, 1])
        T = place("T", [P, 2, S])
        SQ = place("SQ", [P, 2, S])
        RN = place("RN", [P, 6, TC])
        DIAG = T[:, 0, :]
        low = top[0]
        put = arena(low)
        HIDH = put("HIDH", [P, KF, S], F32R)
        HIDL = put("HIDL", [P, KF, S], F32R)
        put = arena(low)
        SG = place("SG", [P, S], at=(nc.sbuf_usable_end - 4 * S) // 32 * 32)
        RS = place("RS", [P, S], at=(nc.sbuf_usable_end - 4 * S) // 32 * 32 - 4 * S)
        rs_at = (nc.sbuf_usable_end - 4 * S) // 32 * 32 - 4 * S
        assert low + 4 * 2 * KF * S <= rs_at
        EV_YA = put("EV_YA", [P, 4, S])
        EV_XB = put("EV_XB", [P, 4, S])
        EV_GC = put("EV_GC", [P, S])
        EV_U = put("EV_U", [P, S])
        EV_CV = put("EV_CV", [P, S])
        EV_S = put("EV_S", [P, 2, S])
        EV_PD = put("EV_PD", [P, 4, S])
        POOLW = put("POOLW", [P, 4, P])
        put = arena(low)
        XQ = put("XQ", [P, XH, S])
        XK = put("XK", [P, XH, M_MEM])
        XV = put("XV", [P, MC, XH * P])
        XP = put("XP", [P, 2, TC, M_MEM])
        XPT = put("XPT", [P, 2, MC, S])
        XS = put("XS", [P, 2, 3, TC])

        put = arena(low)
        OZ = put("OZ", [P, 18, S])
        MV = put("MV", [P, TC, S])
        QM = put("QM", [96, 8, S])
        KM = put("KM", [96, 8, S])
        VM = put("VM", [P, TC, S])
        MPT = OZ[:, 12:17, :].rearrange("p a b -> p (a b)")
        QR = put("QR", [P, 2, S])
        MP = place("MP", [P, TC, S], at=put.at[0] - 4 * 2 * S)
        MS = place("MS", [P, 3, TC], at=put.at[0] + 4 * 2 * S)
        COS = place("COS", [P, S], at=put.at[0])
        SIN = place("SIN", [P, S], at=put.at[0] + 4 * S)
        RS_OD = VM[:, 0, :]
        put = arena(put.at[0] - 4 * (2 + 4 + 8 + 8) * S)
        LE = put("LE", [P, 1280])
        LW = put("LW", [P, 2, 1280])
        LU = put("LU", [P, 4, S])
        LG = put("LG", [P, TC, 8])
        LT = put("LT", [P, 4, 16])
        LA = put("LA", [P, TC, 4])
        LF = put("LF", [P, TC, 4])
        LL = put("LL", [P, TC, 4])
        LR = put("LR", [4, 4, S])
        LN = put("LN", [P, 8, 16])
        POSI = place("POSI", [P, S], mybir.dt.int32, at=low)
        ANG = place("ANG", [P, 4, S], at=low + 4 * S)

        DEST = {"XQ": XQ, "OZ": OZ, "MV": MV, "QM": QM, "KM": KM, "VM": VM, "QR": QR}

        ident = CON[:, ccol["ident"][0]:ccol["ident"][0] + P]
        mask = CON[:, ccol["mask"][0]:ccol["mask"][0] + P]
        tri = CON[:, ccol["tri"][0]:ccol["tri"][0] + P]
        rot = CON[:, ccol["rot"][0]:ccol["rot"][0] + P]
        freq = CON[:, ccol["freq"][0]:ccol["freq"][0] + 1]
        ident4 = ident.unsqueeze(1).to_broadcast([P, TC, P])

        def par(name, c=0):
            tile = PAR2 if name in param2_columns()[0] else PAR
            return tile[:, pcol[name][0] + c:pcol[name][0] + c + 1]

        ACC = ctx.enter_context(nc.psum_tensor("ACC", [P, 4, S], F32))
        MIX = ctx.enter_context(nc.psum_tensor("MIX", [P, 4, S], F32))

        par_landed = sem("par_landed")
        x_landed = sem("x_landed")
        mem_landed = sem("mem_landed")
        poolw_landed = sem("poolw_landed")
        w_landed = [sem(f"w_landed{i}") for i in range(2)]
        w_hi = sem("w_hi")
        w_lo = sem("w_lo")
        unit_done = sem("unit_done")
        block_done = sem("block_done")
        t_ready = sem("t_ready")
        h_hi = sem("h_hi")
        h_ready = sem("h_ready")
        dve_step = sem("dve_step")
        act_step = sem("act_step")
        ones_ready = sem("ones_ready")
        sq_ready = sem("sq_ready")
        sq_used = sem("sq_used")
        root_ready = sem("root_ready")
        diag_ready = sem("diag_ready")
        scale_ready = sem("scale_ready")
        norm_done = sem("norm_done")
        gate_ready = sem("gate_ready")
        silu_ready = sem("silu_ready")
        hid_hi = sem("hid_hi")
        hid_ready = sem("hid_ready")
        ev_gc = sem("ev_gc")
        pooled = sem("pooled")
        pool_ready = sem("pool_ready")
        xs_scores = sem("xs_scores")
        xs_max = sem("xs_max")
        xs_exp = sem("xs_exp")
        xs_probs = sem("xs_probs")
        xs_turned = sem("xs_turned")
        xs_copied = sem("xs_copied")
        xs_out = sem("xs_out")
        mem_squared = sem("mem_squared")
        mem_summed = sem("mem_summed")
        mem_root = sem("mem_root")
        mem_diag = sem("mem_diag")
        mem_scale = sem("mem_scale")
        out_done = sem("out_done")
        pos_landed = sem("pos_landed")
        angle_ready = sem("angle_ready")
        rope_tables = sem("rope_tables")
        rotated = sem("rotated")
        rope_done = sem("rope_done")
        kr_spread = sem("kr_spread")
        ma_scores = sem("ma_scores")
        ma_max = sem("ma_max")
        ma_exp = sem("ma_exp")
        ma_probs = sem("ma_probs")
        ma_turned = sem("ma_turned")
        ma_copied = sem("ma_copied")
        ma_out = sem("ma_out")
        ml_turned = sem("ml_turned")
        ml_abs = sem("ml_abs")
        ml_log = sem("ml_log")
        ml_ls = sem("ml_ls")
        ml_f = sem("ml_f")
        ml_af = sem("ml_af")
        ml_rows = sem("ml_rows")
        ml_rowsm = sem("ml_rowsm")
        ml_mcol = sem("ml_mcol")
        ml_em = sem("ml_em")
        ml_bcast = sem("ml_bcast")
        ml_scores = sem("ml_scores")
        ml_decay = sem("ml_decay")
        ml_sw = sem("ml_sw")
        ml_num = sem("ml_num")
        ml_u = sem("ml_u")
        ml_usq = sem("ml_usq")
        ml_ssq = sem("ml_ssq")
        ml_sig = sem("ml_sig")
        ml_var = sem("ml_var")
        ml_root = sem("ml_root")
        ml_diag = sem("ml_diag")
        par2_landed = sem("par2_landed")
        cv_center = sem("cv_center")
        cv_done = sem("cv_done")
        silu_done = sem("silu_done")
        dn_sq = sem("dn_sq")
        dn_ssq = sem("dn_ssq")
        dn_root = sem("dn_root")
        dn_var = sem("dn_var")
        dn_diag = sem("dn_diag")
        dn_scale = sem("dn_scale")
        dn_kn = sem("dn_kn")
        dn_g16 = sem("dn_g16")
        dn_ge = sem("dn_ge")
        dn_gv = sem("dn_gv")
        dn_gc = sem("dn_gc")
        dn_gb = sem("dn_gb")
        dn_kq = sem("dn_kq")
        dn_tok = sem("dn_tok")
        dn_e1 = sem("dn_e1")
        dn_dg = sem("dn_dg")
        dn_dt = sem("dn_dt")
        dn_kv = sem("dn_kv")
        dn_at = sem("dn_at")
        dn_qd = sem("dn_qd")
        dn_kgd = sem("dn_kgd")
        dn_b = sem("dn_b")
        dn_x = sem("dn_x")
        dn_y = sem("dn_y")
        dn_yc = sem("dn_yc")
        dn_t = sem("dn_t")
        dn_uw = sem("dn_uw")
        dn_wt = sem("dn_wt")
        dn_ub = sem("dn_ub")
        dn_w = sem("dn_w")
        dn_vn = sem("dn_vn")
        dn_upd = sem("dn_upd")
        dn_s = sem("dn_s")
        dn_o = sem("dn_o")
        dn_oc = sem("dn_oc")
        hy_w = sem("hy_w")
        hy_wo = sem("hy_wo")
        hy_m = sem("hy_m")
        hy_mi = sem("hy_mi")
        hy_lin = sem("hy_lin")
        hy_arg = sem("hy_arg")
        hy_sin = sem("hy_sin")
        hy_zero = sem("hy_zero")
        hy_dec = [sem(f"hy_dec{i}") for i in range(2)]
        hy_f = sem("hy_f")
        hy_fd = sem("hy_fd")
        hy_sp = sem("hy_sp")
        hy_odd = sem("hy_odd")
        hy_spd = sem("hy_spd")
        hy_zt = sem("hy_zt")
        hy_ztc = sem("hy_ztc")
        hy_a = sem("hy_a")
        hy_y = sem("hy_y")
        hy_z = sem("hy_z")
        ml_scale = sem("ml_scale")

        def periods(eng, st, body):
            n = -(-st.nb // (2 * st.bpu))
            lo = 1 if st.opens else 0
            hi = n - 1 if st.last or st.nb % (2 * st.bpu) else n
            for i in range(lo):
                body(i)
            if hi - lo > 2:
                with eng.Fori(lo, hi) as i:
                    body(i)
            else:
                for i in range(lo, hi):
                    body(i)
            for i in range(max(hi, lo), n):
                body(i)

        class Steps:

            def __init__(self, eng, s):
                self.eng, self.sem, self.n = eng, s, 0

            def __call__(self, ins):
                self.n = self.n + 1
                ins.then_inc(self.sem, 1)
                self.eng.wait_ge(self.sem, self.n)

        def in_period(st, i):
            per = 2 * st.bpu
            return range(min(per, st.nb - i * per) if isinstance(i, int) else per)

        def unit_of(st, i, j):
            return st.u0 + j, i * (2 * st.upb)

        def done_after(st, i, j):
            n, add = unit_of(st, i, (j // st.bpu + 1) * st.upb)
            return n + add

        pcol2, n_par2 = param2_columns()
        ccol2, cvals2 = const2_columns()
        PAR2 = place("PAR2", [P, n_par2], at=mem_at)
        CON2 = place("CON2", [P, cvals2.shape[1]], at=mem_at + (4 * n_par2 + 31) // 32 * 32)
        assert 4 * (n_par2 + cvals2.shape[1]) + 32 < 4 * KD * M_MEM
        levels = CON2[:, 0:7 * P].rearrange("p (l n) -> p l n", l=7)
        triT = CON2[:, ccol2["triT"][0]:ccol2["triT"][0] + P]
        put = arena(low)
        HY = put("HY", [P, 12, S])
        hy_low = put.at[0]
        DQ = put("DQ", [P, 12, S])
        DZ = put("DZ", [P, 5, S])
        E1 = put("E1", [P, 2, TC, P])
        DT = put("DT", [P, 2, TC, P])
        KV = put("KV", [P, 2, TC, P])
        ST = put("ST", [P, 2, 2, P])
        G16 = put("G16", [P, TC, 16])
        GT = put("GT", [P, 12, 2, TC, 4])
        GL = put("GL", [P, 6, TC, 8])
        RQ = put("RQ", [P, 6, 32])
        WO = put("WO", [P, 8, 16])
        cvt_at = put.at[0]
        CVT = put("CVT", [P, 2, 2, S])
        WMLP = put("WMLP", [64, 192])
        assert put.at[0] <= rs_at
        put = arena(hh_at)
        XI = put("XI", [P, 2, TC, P])
        XIT = put("XIT", [P, 2, TC, P])
        YS = put("YS", [P, 2, TC, P])
        AT = put("AT", [P, 2, TC, P])
        BL = put("BL", [P, 2, 2, TC, P])
        KG = put("KG", [P, 2, TC, P])
        KD_ = put("KD_", [P, 2, TC, P])
        E1B = place("E1B", [P, 2, TC, P], at=cvt_at)
        ATB = place("ATB", [P, 2, TC, P], at=cvt_at + 4 * TC * P * 2)
        E1S, ATS = (E1, E1B), (AT, ATB)
        WT = XI
        UB = YS
        put = arena(hy_low)
        FWD = put("FWD", [P, 2, 2, 2, 256])
        INV = put("INV", [P, 2, 2, 2, 256])
        KS = put("KS", [P, 2, 4, S])
        ZS = put("ZS", [P, 2, 4, S])
        FS = put("FS", [P, 2, 4, S])
        WOUT = put("WOUT", [64, 2, S])
        hd_at = mem_at + (4 * n_par2 + 31) // 32 * 32 + 4 * cvals2.shape[1]
        HD = place("HD", [64, S + 1], at=hd_at)
        assert hd_at + 4 * (S + 8) <= mem_at + 4 * KD * M_MEM
        ZT = FS[:, 0]
        DEC = place("DEC", [P, 2, 2, S], at=hh_at + 4 * 4 * S)
        PT2 = place("PT2", [P, 4, S], at=hh_at + 4 * 4 * S)
        YT = place("YT", [P, 4, S], at=hl_at + 4 * 4 * S)
        FEAT = place("FEAT", [33, S], at=(nc.sbuf_usable_end - 4 * S) // 32 * 32)
        DEST.update({"DQ": DQ, "DZ": DZ, "HY": HY})
        for n, (at, w) in pcol2.items():
            pcol[n] = (at, w)

        COFF = [0, 512, 1024, 896]

        block = ctx.enter_context(nc.Block())

        @block.sync
        def _(sp):
            sp.dma_start(X[:], xT).then_inc(x_landed, 16)

            def load(st, i, j):
                n, add = unit_of(st, i, j)
                if not (isinstance(i, int) and n + add < 2):
                    sp.wait_ge(w_hi, n + add - 1)
                    sp.wait_ge(w_lo, n + add - 1)
                tiles = TILES
                if st.upb > 1 and j % st.upb == st.upb - 1:
                    tiles = 2 * (st.kc - 8 * (st.upb - 1))
                elif st.bpu == 1 and st.kc < 8:
                    tiles = 2 * st.kc
                sp.dma_start(RAW[n % 2][:, 0:tiles * P], wall[bass.ds(n + add, 1), :, 0:tiles * P])\
                    .then_inc(w_landed[n % 2], 16)

            for st in stages:
                if st.kind == "linear":
                    periods(sp, st, lambda i: [load(st, i, j) for j in range(len(in_period(st, i)) * st.upb // st.bpu)])
            sp.wait_ge(block_done, n_blocks)
            sp.wait_ge(norm_done, stages[-1].plain + (stages[-1].kind == "rms"))
            sp.dma_start(out, X[:]).then_inc(out_done, 16)
            sp.wait_ge(out_done, 16)

        @block.gpsimd
        def _(pool):
            pool.dma_start(PAR[:], params).then_inc(par_landed, 16)
            pool.dma_start(CON[:], consts).then_inc(par_landed, 16)
            pool.dma_start(MEM[:], memT).then_inc(mem_landed, 16)
            pool.dma_start(POOLW[:], poolw).then_inc(poolw_landed, 16)
            for st in stages:
                if st.kind == "rope":
                    pool.wait_ge(block_done, st.b0 - 2)
                    pool.dma_start(POSI[:], pos).then_inc(pos_landed, 16)
                if st.kind == "linear" and st.name == "ffn1_gu":
                    pool.wait_ge(block_done, st.b0)
                    pool.dma_start(PAR2[:], params2).then_inc(par2_landed, 16)
                    pool.dma_start(CON2[:], consts2).then_inc(par2_landed, 16)
                if st.kind == "delta":
                    wout = filters[st.layer][:, 192:].rearrange("p (b o n) -> p o b n", b=2, o=2)
                    pool.wait_ge(block_done, st.b0)
                    pool.wait_ge(hy_arg, 3 * st.layer + 3)
                    pool.dma_start(WOUT[:], wout[:, 0]).then_inc(hy_wo, 16)
                    for h in range(4):
                        o = 4 * st.layer + h
                        pool.wait_ge(dn_at, o + 1)
                        for l in range(7):
                            if l >= 2:
                                pool.wait_ge(dn_y, 14 * o + 2 * (l - 1))
                            if l == 2:
                                pool.wait_ge(dn_x, 14 * o + 2)
                            m = levels[:, l, :].unsqueeze(1).to_broadcast([P, 2 * TC, P])
                            pool.tensor_tensor(BL[:, l % 2].rearrange("p d c n -> p (d c) n"),
                                               DT[:].rearrange("p d c n -> p (d c) n"), m, ALU.mult).then_inc(dn_b, 1)
                if st.kind == "net" and st.step == 0:
                    pool.wait_ge(block_done, st.b0 - 6)
                    pool.dma_start(WMLP[:], filters[st.layer][:, 0:192]).then_inc(hy_w, 16)
                    pool.dma_start(FEAT[:], feats).then_inc(hy_w, 16)
                if st.kind == "hyena":
                    l = st.layer
                    pool.wait_ge(h_ready, st.h0)
                    wout = filters[l][:, 192:].rearrange("p (b o n) -> p o b n", b=2, o=2)
                    for o in range(2):
                        if o:
                            pool.wait_ge(hy_f, 8 * l + 4)
                            pool.dma_start(WOUT[:], wout[:, 1]).then_inc(hy_wo, 16)
                        for q in range(4):
                            n = 8 * l + 4 * o + q
                            if q < 2 and n >= 4:
                                pool.wait_ge(hy_z, 8 * l + 4 * o)
                            if q >= 2:
                                pool.wait_ge(hy_fd, n - 1)
                            pool.dma_start(DEC[:, q % 2], decays[:, q]).then_inc(hy_dec[q % 2], 16)
                            if n % 8 == 1:
                                pool.dma_start(FWD[:].rearrange("p a b c d -> p (a b c d)"), mats[:, 0:2048]).then_inc(hy_m, 16)
                                pool.dma_start(INV[:].rearrange("p a b c d -> p (a b c d)"), mats[:, 2048:4096]).then_inc(hy_mi, 16)

        @block.tensor
        def _(pe):
            def three(out_ap, wh, wl, hh, hl, first, last):
                pe.matmul(out_ap, wh, hh, start=first, stop=False)
                pe.matmul(out_ap, wh, hl, start=False, stop=False)
                return pe.matmul(out_ap, wl, hh, start=False, stop=last)

            def pe_linear(st):
                src_h, src_l = (HIDH, HIDL) if st.out == "resid" and st.src == "hid" else (HH, HL)
                width = M_MEM if st.out == "fm_mem" else S
                tcs = {"tm": TC, "tm_mem": MC}.get(st.out, 0)

                def period(i):
                    upp = 2 * st.upb
                    bpp = 2 * st.bpu
                    for j in in_period(st, i):
                        b = i * bpp + (st.b0 + j)
                        pair = (st.b0 + j) % 2
                        first_block = st.opens and isinstance(i, int) and i == j == 0
                        second_block = st.opens and isinstance(i, int) and i == 0 and j == 1
                        if not (isinstance(i, int) and b < 2):
                            pe.wait_ge(block_done, b - 1)
                        for q in range(st.upb):
                            ju = j * st.upb + q if st.bpu == 1 else j // st.bpu
                            n, add = unit_of(st, i, ju)
                            slot = n % 2
                            pe.wait_ge(w_lo, n + add + 1)
                            ks = range(8 * q, min(8 * q + 8, st.kc))
                            t0 = (j % st.bpu) * 2 * st.kc
                            if first_block and not tcs:
                                for k in ks:
                                    pe.wait_ge(h_ready, st.hin + k + 1)
                                    for m in range(2):
                                        c0 = (t0 + 2 * k + m) * P
                                        last = three(ACC[:, 2 * pair + m, :], WH[slot][:, c0:c0 + P], WL[slot][:, c0:c0 + P],
                                                     HH[:, k, :], HL[:, k, :], k == 0, k == st.kc - 1)
                            elif tcs:
                                for tc in range(tcs):
                                    if second_block and tc == 2:
                                        late_scale(st.norm)
                                    for k in ks:
                                        if tc == 0 and not st.whole:
                                            pe.wait_ge(h_ready, st.hin + k + 1)
                                        o = ACC[:, 2 * pair:2 * pair + 2, :].rearrange("p a (b n) -> p (a b) n", b=2)[:, tc]
                                        th, tl = HH[:, st.k0 + k, tc * P:tc * P + P], HL[:, st.k0 + k, tc * P:tc * P + P]
                                        c0 = (t0 + 2 * (k - 8 * q)) * P
                                        wh, wl = WH[slot][:, c0:c0 + 256], WL[slot][:, c0:c0 + 256]
                                        last = three(o, th, tl, wh, wl, k == 0, k == st.kc - 1)
                            else:
                                for m in range(1 if st.half and isinstance(i, int) and i * bpp + j == st.nb - 1 else 2):
                                    if second_block and m == 1:
                                        late_scale(st.norm)
                                    for k in ks:
                                        if m == 0 and src_h is HH and not st.whole:
                                            pe.wait_ge(h_ready, st.hin + k + 1)
                                        if m == 0 and src_h is HIDH:
                                            pe.wait_ge(hid_ready, st.hidin + k + 1)
                                        c0 = (t0 + 2 * (k - 8 * q) + m) * P
                                        last = three(ACC[:, 2 * pair + m, 0:width],
                                                     WH[slot][:, c0:c0 + P], WL[slot][:, c0:c0 + P],
                                                     src_h[:, st.k0 + k, 0:width], src_l[:, st.k0 + k, 0:width],
                                                     k == 0, k == st.kc - 1)
                            if j % st.bpu == st.bpu - 1:
                                last.then_inc(unit_done, 1)
                        if first_block and st.norm.own == 2:
                            sum_squares(st.norm, range(st.norm.n - 2, st.norm.n))
                        if st.feeds and b > st.b0:
                            c = 2 * (b - st.b0 - 1)
                            sum_squares(st.feeds, range(c, c + 2))
                if st.whole:
                    pe.wait_ge(h_ready, st.hall)
                periods(pe, st, period)

            def sum_squares(st, chunks):
                for c in chunks:
                    pe.wait_ge(sq_ready, st.sq0 + c + 1)
                    if c == 0 and st.plain:
                        pe.wait_ge(norm_done, st.plain)
                    for tc in range(TC):
                        mm = pe.matmul(MIX[:, 0, tc:tc + 1], SQ[:, (st.sq0 + c) % 2, tc * P:tc * P + P], ONES[:, 0:1],
                                       start=(c == 0 and tc == 0), stop=(c == st.n - 1), skip_group_check=True)
                    mm.then_inc(sq_used, 1)

            def late_scale(st):
                pe.wait_ge(diag_ready, st.nrm + 1)
                pe.matmul(MIX[:, 1, :], ONES[:], DIAG, start=True, stop=True).then_inc(scale_ready, 1)

            def pe_norm(st):
                if st.gain == "ffn1n0":
                    pe.wait_ge(par2_landed, 32)
                if not st.late or st.own == st.n:
                    sum_squares(st, range(st.n - st.own, st.n))
                if not st.late:
                    late_scale(st)

            def pe_mem(st):
                if st.nth:
                    return
                for c in range(KD):
                    pe.wait_ge(mem_squared, c + 1)
                    for mc in range(MC):
                        mm = pe.matmul(MIX[:, 0, mc:mc + 1], SQ[:, c % 2, mc * P:mc * P + P], ONES[:, 0:1],
                                       start=(c == 0 and mc == 0), stop=(c == KD - 1), skip_group_check=True)
                    mm.then_inc(mem_summed, 1)
                pe.wait_ge(mem_diag, 1)
                pe.matmul(MIX[:, 1, 0:M_MEM], ONES[:], DIAG[:, 0:M_MEM], start=True, stop=True).then_inc(mem_scale, 1)

            def pe_even(st):
                pe.wait_ge(poolw_landed, 16)
                for g in range(4):
                    pe.wait_ge(pooled, g + 1)
                    pe.matmul(MIX[:, g, :], POOLW[:, g, :], EV_PD[:, g, :], start=True, stop=True)\
                        .then_inc(pool_ready, 1)

            def pe_xattn(st):
                o = st.nth * XH

                def scores(h):
                    if h == 0:
                        pe.wait_ge(block_done, st.b0)
                    if h >= 2:
                        pe.wait_ge(xs_exp, o + h - 1)
                    for tc in range(TC):
                        dst = ACC[:, 2 * (h % 2):2 * (h % 2) + 2, :].rearrange("p a (b n) -> p (a b) n", b=2)[:, tc]
                        mm = pe.matmul(dst, XQ[:, h, tc * P:tc * P + P], XK[:, h, :], start=True, stop=True)
                    mm.then_inc(xs_scores, 1)

                def turn(h):
                    pe.wait_ge(xs_probs, o + h + 1)
                    if h >= 1:
                        pe.wait_ge(xs_copied, o + h)
                    for mc in range(MC):
                        for tc in range(TC):
                            mm = pe.transpose(MIX[:, mc, tc * P:tc * P + P],
                                              XP[:, h % 2, tc, mc * P:mc * P + P], ident)
                    mm.then_inc(xs_turned, 1)

                def output(h):
                    pe.wait_ge(xs_copied, o + h + 1)
                    if h >= 2:
                        pe.wait_ge(t_ready, st.h0 + h - 1)
                    for mc in range(MC):
                        mm = pe.matmul(MIX[:, 2 + h % 2, :], XV[:, mc, h * P:h * P + P], XPT[:, h % 2, mc, :],
                                       start=(mc == 0), stop=(mc == MC - 1))
                    mm.then_inc(xs_out, 1)

                scores(0)
                for h in range(XH):
                    if h + 1 < XH:
                        scores(h + 1)
                    turn(h)
                    if h:
                        output(h - 1)
                output(XH - 1)

            def pe_delta(st):
                L = st.layer
                ssq = MIX[:, 2, 0:32]
                for m in range(8):
                    pe.wait_ge(dn_sq, 12 * L + m + 1)
                    if m == 0:
                        pe.wait_ge(block_done, st.b0)
                    for tc in range(TC):
                        mm = pe.matmul(MIX[:, 2, 4 * m + tc:4 * m + tc + 1], SQ[:, m % 2, tc * P:tc * P + P], ONES[:, 0:1],
                                       start=True, stop=True)
                    mm.then_inc(dn_ssq, 1)
                for tc in range(TC):
                    mm = pe.transpose(MIX[:, 3, 16 * tc:16 * tc + 16], DZ[0:16, 4, tc * P:tc * P + P], ident[0:16, 0:16])
                mm.then_inc(dn_g16, 1)
                for h in range(4):
                    pe.wait_ge(dn_diag, 8 * L + h + 1)
                    if h >= 2:
                        pe.wait_ge(dn_kn, 4 * L + h - 1)
                    pe.matmul(MIX[:, h % 2, :], ONES[:], T[:, h % 2, :], start=True, stop=True).then_inc(dn_scale, 1)
                pe.wait_ge(dn_gv, 2 * L + 2)
                g8 = GL[:, 3]
                pe.matmul(MIX[:, 3, 64:80], tri, g8[:, :, 0:4], start=True, stop=True)
                pe.matmul(MIX[:, 3, 80:96], triT, g8[:, :, 4:8], start=True, stop=True)
                pe.matmul(MIX[:, 3, 96:128], ONES[:], g8, start=True, stop=True).then_inc(dn_gc, 1)
                pe.wait_ge(dn_kn, 4 * L + 4)
                def sums_of_g(h):
                    for d in range(2):
                        for c in range(TC):
                            mm = pe.matmul(ACC[:, d, c * P:c * P + P], g8[:, c, 4 * d + h:4 * d + h + 1].to_broadcast([P, P]),
                                           tri if d == 0 else triT, start=True, stop=True)
                    mm.then_inc(dn_gb, 1)

                def products(h):
                    for c in range(TC):
                        cs = slice(c * P, c * P + P)
                        mm = pe.matmul(ACC[:, 2 + c // 2, 256 * (c % 2):256 * (c % 2) + 256], DQ[:, 4 + h, cs],
                                       DQ[:, h:h + 5:4, cs], start=True, stop=True)
                    mm.then_inc(dn_kq, 1)

                def turn(h):
                    if h == 0:
                        pe.wait_ge(silu_done, 2 * L + 2)
                    for c in range(TC):
                        pe.transpose(MIX[:, 0, c * P:c * P + P], DQ[:, 4 + h, c * P:c * P + P], ident)
                        mm = pe.transpose(MIX[:, 1, c * P:c * P + P], DQ[:, 8 + h, c * P:c * P + P], ident)
                    mm.then_inc(dn_tok, 1)

                sums_of_g(0)
                products(0)
                turn(0)
                for h in range(4):
                    o = 4 * L + h
                    pe.wait_ge(dn_e1, o + 1)
                    pe.wait_ge(dn_b, 7 * o + 1)
                    pe.wait_ge(dn_kv, o + 1)
                    for d in range(2):
                        for c in range(TC):
                            mm = pe.transpose(MIX[:, d, c * P:c * P + P], BL[:, 0, d, c, :], ident)
                        mm.then_inc(dn_y, 1)
                    for l in range(1, 7):
                        for d in range(2):
                            pe.wait_ge(dn_x, 14 * o + 2 * (l - 1) + d + 1)
                            pe.wait_ge(dn_b, 7 * o + l + 1)
                            for c in range(TC):
                                mm = pe.matmul(ACC[:, d, c * P:c * P + P], BL[:, l % 2, d, c, :], XI[:, d, c, :], start=True, stop=True)
                            mm.then_inc(dn_y, 1)
                        for d in range(2):
                            pe.wait_ge(dn_yc, 12 * o + 2 * (l - 1) + d + 1)
                            tb, ttb = (ACC[:, 2], ACC[:, 3]) if d == 0 else (MIX[:, 0], MIX[:, 1])
                            for c in range(TC):
                                if l < 6:
                                    pe.matmul(tb[:, c * P:c * P + P], XIT[:, d, c, :], YS[:, d, c, :], start=True, stop=True)
                                mm = pe.matmul(ttb[:, c * P:c * P + P], YS[:, d, c, :], XIT[:, d, c, :], start=True, stop=True)
                            mm.then_inc(dn_t, 1)
                    pe.wait_ge(dn_x, 14 * o + 14)
                    pe.wait_ge(dn_kgd, o + 1)
                    for d in range(2):
                        for c in range(TC):
                            pe.matmul(ACC[:, d, c * P:c * P + P], XIT[:, d, c, :], KV[:, 1, c, :], start=True, stop=True)
                            mm = pe.matmul(ACC[:, 2 + d, c * P:c * P + P], KG[:, d, c, :], XIT[:, d, c, :], start=True, stop=True)
                    mm.then_inc(dn_uw, 1)
                    pe.wait_ge(dn_ub, o + 1)
                    if h < 3:
                        sums_of_g(h + 1)
                    pe.wait_ge(dn_wt, o + 1)
                    if h:
                        pe.wait_ge(dn_oc, o)
                    for s in range(TC):
                        at = (s, TC - 1 - s)
                        if s == 1 and h < 3:
                            products(h + 1)
                        if s == 2 and h < 3:
                            turn(h + 1)
                        if s:
                            pe.wait_ge(dn_s, 3 * o + s)
                            for d in range(2):
                                mm = pe.matmul(MIX[:, 2, d * P:d * P + P], WT[:, d, at[d], :], ST[:, (s - 1) % 2, d, :], start=True, stop=True)
                            mm.then_inc(dn_w, 1)
                            pe.wait_ge(dn_vn, 3 * o + s)
                        if s < TC - 1:
                            for d in range(2):
                                mm = pe.matmul(MIX[:, 2, 256 + d * P:256 + d * P + P], KD_[:, d, at[d], :], UB[:, d, at[d], :],
                                               start=True, stop=True)
                            mm.then_inc(dn_upd, 1)
                        for d in range(2):
                            dst = MIX[:, 3, at[d] * P:at[d] * P + P]
                            if s:
                                pe.matmul(dst, ST[:, (s - 1) % 2, d, :], E1S[h % 2][:, d, at[d], :], start=False, stop=False, skip_group_check=True)
                            mm = pe.matmul(dst, UB[:, d, at[d], :], ATS[h % 2][:, d, at[d], :], start=(s == 0 and d == 0),
                                           stop=(s == TC - 1), skip_group_check=True)
                    mm.then_inc(dn_o, 1)
                for h in range(4):
                    pe.wait_ge(dn_sq, 12 * L + 8 + h + 1)
                    if h == 0:
                        pe.wait_ge(dn_oc, 4 * L + 4)
                    for tc in range(TC):
                        mm = pe.matmul(MIX[:, 2, 4 * h + tc:4 * h + tc + 1], SQ[:, h % 2, tc * P:tc * P + P], ONES[:, 0:1],
                                       start=True, stop=True)
                    mm.then_inc(dn_ssq, 1)
                for h in range(4):
                    pe.wait_ge(dn_diag, 8 * L + 4 + h + 1)
                    if h >= 2:
                        pe.wait_ge(t_ready, st.h0 + h - 1)
                    pe.matmul(MIX[:, h % 2, :], ONES[:], KV[:, h % 2].rearrange("p c n -> p (c n)"), start=True, stop=True)\
                        .then_inc(dn_scale, 1)

            def pe_net(st):
                n = 3 * st.layer + st.step
                if st.step == 0:
                    pe.wait_ge(hy_w, 32 * (st.layer + 1))
                    rhs, rows = FEAT[:], 33
                else:
                    pe.wait_ge(hy_sin, n)
                    rhs, rows = T[0:64, 1, :], 64
                pe.matmul(MIX[0:64, 2, :], WMLP[0:rows, 64 * st.step:64 * st.step + 64], rhs, start=True, stop=True)\
                    .then_inc(hy_lin, 1)

            def pe_hyena(st):
                L = st.layer
                pe.wait_ge(hy_sin, 3 * L + 3)
                pe.wait_ge(hy_zero, L + 1)

                def spectrum(n, a, b):
                    for fc, bank in ((0, ACC), (1, MIX)):
                        for cs, src in ((0, a), (1, b)):
                            for p in range(2):
                                for kc in range(2):
                                    mm = pe.matmul(bank[:, 2 * cs + p, :], FWD[:, cs, p, kc, fc * P:fc * P + P],
                                                   src[:, 2 * p + kc, :], start=(kc == 0), stop=(kc == 1))
                        mm.then_inc(hy_sp, 1)

                for o in range(2):
                    n = 2 * L + o
                    pe.wait_ge(hy_wo, 16 * (n + 1))
                    for q in range(4):
                        p, kc = q // 2, q % 2
                        if q >= 2 or o:
                            pe.wait_ge(hy_fd, 4 * n + q - 1 if q >= 2 else 4 * n)
                        if q < 2 and o:
                            pe.wait_ge(hy_spd, 4 * n)
                        for back in range(2):
                            first = 1 - back + p + 2 * P * kc
                            mm = pe.matmul(ACC[:, 2 * (q % 2) + back, :], HD[:, first:first + 2 * P - 1:2],
                                           WOUT[:, back, :], start=True, stop=True)
                        mm.then_inc(hy_f, 1)
                    pe.wait_ge(hy_fd, 4 * n + 4)
                    pe.wait_ge(hy_m, 16 * (L + 1))
                    spectrum(2 * n, FS[:, 0], FS[:, 1])
                    pe.wait_ge(hy_spd, 4 * n + 2)
                    if o:
                        pe.wait_ge(hy_z, 8 * L + 4)
                    for q in range(4):
                        p, kc = q // 2, q % 2
                        for m in range(4):
                            first = p + 2 * P * kc
                            mm = pe.transpose(ACC[:, q, m * P:m * P + P], HY[:, m, first:first + 2 * P - 1:2], ident)
                    mm.then_inc(hy_zt, 1)
                    pe.wait_ge(hy_ztc, n + 1)
                    spectrum(2 * n + 1, ZT, ZT)
                    pe.wait_ge(hy_mi, 16 * (L + 1))
                    for fc in range(2):
                        pe.wait_ge(hy_a, 2 * n + fc + 1)
                        for m in range(4):
                            for p in range(2):
                                for cs in range(2):
                                    mm = pe.matmul(MIX[:, m, 256 * p:256 * p + 256], ZS[:, fc, 2 * p + cs, m * P:m * P + P],
                                                   INV[:, cs, p, fc, :], start=(fc == cs == p == 0), stop=(fc == 1 and cs == 1),
                                                   skip_group_check=True)
                            if fc:
                                mm.then_inc(hy_y, 1)

            def pe_mla(st):
                pe.wait_ge(block_done, st.b0)
                for m in range(2):
                    pe.matmul(MIX[:, m, :], rot, QR[:, m, :], start=True, stop=True).then_inc(rotated, 1)
                pe.matmul(MIX[0:32, 2, :], rot[0:32, 0:32], OZ[0:32, 17, :], start=True, stop=True).then_inc(rotated, 1)

                def scores(h):
                    if h == 0:
                        pe.wait_ge(rope_done, 3)
                        pe.wait_ge(kr_spread, 1)
                    else:
                        pe.wait_ge(ma_exp, h)
                    for tc in range(TC):
                        n = P * (tc + 1)
                        pe.matmul(ACC[:, tc, 0:n], QM[:, h, tc * P:tc * P + P], KM[:, h, 0:n], start=True, stop=False)
                        mm = pe.matmul(ACC[:, tc, n - P:n], ident, mask, start=False, stop=True)
                    mm.then_inc(ma_scores, 1)

                def turn(h):
                    pe.wait_ge(ma_probs, h + 1)
                    if h:
                        pe.wait_ge(ma_copied, h)
                    for kc in range(TC):
                        for tc in range(kc, TC):
                            at = COFF[kc] + (tc - kc) * P
                            mm = pe.transpose(MIX[:, at // S, at % S:at % S + P], MP[:, tc, kc * P:kc * P + P], ident)
                    mm.then_inc(ma_turned, 1)

                def output(h):
                    pe.wait_ge(ma_copied, h + 1)
                    if h >= 2 and h % 2 == 0:
                        pe.wait_ge(t_ready, st.h0 + h // 2)
                    rows = slice(64 * (h % 2), 64 * (h % 2) + 64)
                    for kc in range(TC):
                        mm = pe.matmul(MIX[rows, 3, kc * P:S], VM[:, kc, 64 * h:64 * h + 64],
                                       MPT[:, 1280 * (h % 2) + COFF[kc]:1280 * (h % 2) + COFF[kc] + S - kc * P],
                                       start=(kc == 0), stop=(kc == TC - 1), skip_group_check=True)
                    mm.then_inc(ma_out, 1)

                scores(0)
                for h in range(8):
                    if h < 7:
                        scores(h + 1)
                    turn(h)
                    output(h)

            def pe_mlstm(st):
                for tc in range(TC):
                    mm = pe.transpose(MIX[:, 0, 8 * tc:8 * tc + 8], OZ[32:40, 17, tc * P:tc * P + P], ident[32:40, 32:40])
                mm.then_inc(ml_turned, 1)
                pe.wait_ge(ml_ls, 1)
                for j in range(TC):
                    for i in range(j + 1):
                        mm = pe.matmul(MIX[:, 1, 4 * j:4 * j + 4], tri if i == j else ONES[:], LL[:, i, :],
                                       start=(i == 0), stop=(i == j))
                mm.then_inc(ml_f, 1)
                pe.wait_ge(ml_af, 1)
                for tc in range(TC):
                    pe.transpose(MIX[0:4, 2, tc * P:tc * P + P], LA[:, tc, :], ident)
                    mm = pe.transpose(MIX[0:4, 3, tc * P:tc * P + P], LF[:, tc, :], ident)
                mm.then_inc(ml_rows, 1)
                pe.wait_ge(ml_rowsm, 1)
                for tc in range(TC):
                    mm = pe.transpose(MIX[:, 0, 4 * tc:4 * tc + 4], LR[:, 3, tc * P:tc * P + P], ident[0:4, 0:4])
                mm.then_inc(ml_mcol, 1)
                pe.wait_ge(ml_em, 1)

                def head(h):
                    if h:
                        pe.wait_ge(ml_decay, h)
                    pe.matmul(MIX[:, 0, :], ident[0:4, h:h + 1].to_broadcast([4, P]), LR[:, 2, :], start=True, stop=True)
                    pe.matmul(MIX[:, 1, :], ident[0:4, h:h + 1].to_broadcast([4, P]), LR[:, 2, :], start=True, stop=False)
                    pe.matmul(MIX[:, 1, :], mask, ident4, start=False, stop=True).then_inc(ml_bcast, 1)
                    if h:
                        pe.wait_ge(ml_sw, h)
                    for kc in range(TC):
                        a, n = COFF[kc], S - kc * P
                        mm = pe.matmul(ACC[:, a // S, a % S:a % S + n], OZ[:, 4 + h, kc * P:kc * P + P],
                                       OZ[:, h, kc * P:S], start=True, stop=True)
                    mm.then_inc(ml_scores, 1)

                def sums(h):
                    pe.wait_ge(ml_sw, h + 1)
                    for tc in range(TC):
                        for kc in range(tc + 1):
                            a = COFF[kc] + (tc - kc) * P
                            pe.matmul(MIX[:, 2, 4 * tc + h:4 * tc + h + 1], LW[:, h % 2, a:a + P], ONES[:, 0:1],
                                      start=(kc == 0), stop=(kc == tc))
                    if h:
                        pe.wait_ge(ml_u, h)
                    for kc in range(TC):
                        mm = pe.matmul(MIX[:, 3, kc * P:S], MV[:, kc, h * P:h * P + P],
                                       LW[:, h % 2, COFF[kc]:COFF[kc] + S - kc * P], start=(kc == 0), stop=(kc == TC - 1),
                                       skip_group_check=True)
                    mm.then_inc(ml_num, 1)

                def squares(h):
                    pe.wait_ge(ml_usq, h + 1)
                    for tc in range(TC):
                        mm = pe.matmul(MIX[:, 2, 16 + 4 * tc + h:17 + 4 * tc + h], SQ[:, h % 2, tc * P:tc * P + P], ONES[:, 0:1],
                                       start=True, stop=True)
                    mm.then_inc(ml_ssq, 1)

                head(0)
                for h in range(4):
                    if h < 3:
                        head(h + 1)
                    sums(h)
                    if h:
                        squares(h - 1)
                squares(3)
                for h in range(4):
                    pe.wait_ge(ml_diag, h + 1)
                    if h >= 2:
                        pe.wait_ge(t_ready, st.h0 + h - 1)
                    pe.matmul(MIX[:, h % 2, :], ONES[:], LE[:, 512 * (h % 2):512 * (h % 2) + 512], start=True, stop=True).then_inc(ml_scale, 1)

            pe.wait_ge(par_landed, 32)
            pe.wait_ge(ones_ready, 1)
            for st in stages:
                {"linear": pe_linear, "norm": pe_norm, "rms": pe_norm, "mem": pe_mem,
                 "even": pe_even, "xattn": pe_xattn, "rope": lambda st: None, "mla": pe_mla, "mlstm": pe_mlstm,
                 "net": pe_net, "silu_qk": lambda st: None, "delta": pe_delta, "hyena": pe_hyena}[st.kind](st)

        @block.scalar
        def _(act):
            step = Steps(act, act_step)

            def split_hi(n, add, i):
                if n >= n_units and isinstance(add, int):
                    return
                act.wait_ge(w_landed[n % 2], add * 8 + 16 * (n // 2 + 1))
                if not (isinstance(i, int) and n + add < 2):
                    act.wait_ge(unit_done, n + add - 1)
                act.activation(WH[n % 2][:], RAW[n % 2][:], ACT.Copy).then_inc(w_hi, 1)

            def act_linear(st):
                def period(i):
                    for j in in_period(st, i):
                        b = i * (2 * st.bpu) + (st.b0 + j)
                        pair = (st.b0 + j) % 2
                        for q in range(st.upb):
                            if st.bpu == 1 or j % st.bpu == 0:
                                n, add = unit_of(st, i, j * st.upb + q if st.bpu == 1 else j // st.bpu)
                                if st.opens and isinstance(i, int) and i == j == 0:
                                    continue
                                if not (st.last and isinstance(i, int) and n + add + 1 >= n_units):
                                    split_hi(n + 1, add, i)
                        if st.feeds and b < st.b0 + st.nb - 1:
                            c = 2 * (b - st.b0)
                            if st.feeds.early:
                                act.wait_ge(unit_done, st.u0)
                                hi_chunks(st.feeds.h0, range(c + 2), first=c)
                            act.wait_ge(block_done, b + 1)
                            square(st.feeds, c)
                            square(st.feeds, c + 1)
                        if st.out == "ffn":
                            act.wait_ge(gate_ready, i * 2 + (st.ffn * KF + j + 1))
                            act.activation(SG[:], SG[:], ACT.Silu).then_inc(silu_ready, 1)
                        if st.out in ("conv5", "conv3"):
                            act.wait_ge(block_done, b + 1)
                            for m in range(2):
                                ch = i * 4 + (2 * j + m)
                                dst = DEST[st.dest][:, bass.ds(ch, 1), :].rearrange("p a n -> p (a n)")
                                if st.out == "conv5":
                                    a = act.activation(dst, CVT[:, j, m, :], ACT.Copy,
                                                       scale=PAR2[:, bass.ds(ch + (pcol[f"conv5{st.layer}"][0] + 24), 1)])
                                else:
                                    a = act.activation(dst, CVT[:, j, m, :], ACT.Identity,
                                                       scale=PAR2[:, bass.ds(ch + (pcol[f"conv3{st.layer}"][0] + 12), 1)],
                                                       bias=PAR2[:, bass.ds(ch + pcol[f"conv3b{st.layer}"][0], 1)])
                            a.then_inc(cv_center, 1)
                        if st.out == "even" and j == 0:
                            act.wait_ge(unit_done, done_after(st, i, j))
                            if not (isinstance(i, int) and b < 1):
                                act.wait_ge(block_done, b)
                            act.activation(EV_GC[:], ACC[:, 2 * pair, :], ACT.Copy).then_inc(ev_gc, 1)
                periods(act, st, period)

            def hi_chunks(h0, dests, width=S, first=0):
                for c, d in list(enumerate(dests))[first:]:
                    act.wait_ge(t_ready, h0 + c + 1)
                    act.activation(HH[:, d, 0:width], T[:, (h0 + c) % 2, 0:width], ACT.Copy).then_inc(h_hi, 1)

            def square(st, c):
                if st.sq0 + c >= 2:
                    act.wait_ge(sq_used, st.sq0 + c - 1)
                src = {"X": X, "Z": OZ, "HY": HY}[st.src]
                act.activation(SQ[:, (st.sq0 + c) % 2, :], src[:, st.c0 + c, :], ACT.Square).then_inc(sq_ready, 1)

            def act_squares(st):
                if st.gain == "final":
                    act.wait_ge(par2_landed, 32)
                if st.gain == "ffn1n0":
                    act.wait_ge(norm_done, st.plain)
                if st.b0 == 0:
                    act.wait_ge(x_landed, 16)
                elif st.src == "HY":
                    act.wait_ge(hy_z, 8 * (st.nrm_hy + 1))
                else:
                    act.wait_ge(block_done, st.b0 if st.gain[:5] != "xattn" else st.b0 - 4)
                for c in range(st.n - st.own, st.n):
                    square(st, c)

            def act_root(st):
                act.wait_ge(sq_used, st.sq0 + st.n)
                act.activation(RN[:, 0, :], MIX[:, 0, 0:TC], ACT.Sqrt, bias=EPSC[:], scale=1.0 / (P * st.n)).then_inc(root_ready, 1)

            def act_norm(st):
                if not st.late:
                    act_squares(st)
                    act_root(st)
                    hi_chunks(st.h0, range(st.d0, st.d0 + st.n))
                    return
                if st.own == st.n:
                    act_squares(st)
                if st.u0:
                    act.wait_ge(unit_done, st.u0)
                hi_chunks(st.h0, range(st.n), first=st.early)
                if st.own < st.n:
                    act_squares(st)
                split_hi(st.u0 + 1, 0, 0)
                act_root(st)

            def act_rms(st):
                act_squares(st)
                act_root(st)

            def act_even(st):
                hi_chunks(st.h0, range(8))

            def act_xattn(st):
                o = st.nth * XH
                for h in range(XH):
                    act.wait_ge(xs_max, o + h + 1)
                    if h >= 2:
                        act.wait_ge(xs_turned, o + h - 1)
                    for tc in range(TC):
                        src = ACC[:, 2 * (h % 2):2 * (h % 2) + 2, :].rearrange("p a (b n) -> p (a b) n", b=2)[:, tc]
                        a = act.activation(XP[:, h % 2, tc, :], src, ACT.Exp, bias=XS[:, h % 2, 0, tc:tc + 1],
                                           scale=float(P) ** -0.5, accum_out=XS[:, h % 2, 1, tc:tc + 1])
                    a.then_inc(xs_exp, 1)
                    if h:
                        copy_turned(st, h - 1)
                    if h >= 2:
                        hi_chunks(st.h0 + h - 2, [h - 2])
                copy_turned(st, XH - 1)
                hi_chunks(st.h0 + XH - 2, [XH - 2, XH - 1])

            def copy_turned(st, h):
                o = st.nth * XH
                act.wait_ge(xs_turned, o + h + 1)
                if h >= 2:
                    act.wait_ge(xs_out, o + h - 1)
                act.activation(XPT[:, h % 2, :, :], MIX[:, 0:2, :], ACT.Copy).then_inc(xs_copied, 1)

            def act_mem(st):
                if st.nth == 0:
                    act_mem_norm(st)
                hi_chunks(st.h0, range(KD), M_MEM)

            def act_mem_norm(st):
                act.wait_ge(mem_landed, 16)
                act.wait_ge(sq_used, st.sq0)
                for c in range(KD):
                    if c >= 2:
                        act.wait_ge(mem_summed, c - 1)
                    act.activation(SQ[:, c % 2, 0:M_MEM], MEM[:, c, :], ACT.Square).then_inc(mem_squared, 1)
                act.wait_ge(mem_summed, KD)
                act.activation(RN[:, 0, 0:MC], MIX[:, 0, 0:MC], ACT.Sqrt, bias=EPSC[:], scale=1.0 / D).then_inc(mem_root, 1)

            def act_silu_qk(st):
                act.wait_ge(cv_done, 12 * st.nth + 6)
                for m in range(4):
                    a = act.activation(DQ[:, 2 * m:2 * m + 2, :], DQ[:, 2 * m:2 * m + 2, :], ACT.Silu)
                a.then_inc(silu_done, 1)

            def act_delta(st):
                L = st.layer
                act.wait_ge(block_done, st.b0)
                act.wait_ge(silu_done, 2 * L + 1)
                for m in range(8):
                    if m >= 2:
                        act.wait_ge(dn_ssq, 12 * L + m - 1)
                    act.activation(SQ[:, m % 2, :], DQ[:, m, :], ACT.Square).then_inc(dn_sq, 1)
                act.activation(DQ[:, 8:12, :], DQ[:, 8:12, :], ACT.Silu).then_inc(silu_done, 1)
                act.wait_ge(dn_var, 2 * L + 1)
                act.activation(RQ[:, 1, :], RQ[:, 0, :], ACT.Sqrt).then_inc(dn_root, 1)
                act.wait_ge(dn_gv, 2 * L + 1)
                act.activation(GL[:, 0], G16[:, :, 0:8], ACT.Sigmoid)
                act.activation(GL[:, 2], GL[:, 1], ACT.Exp, scale=-1.0)
                act.activation(GL[:, 4, 0, :], PAR2[:, pcol[f"alog{L}"][0]:pcol[f"alog{L}"][0] + 8], ACT.Exp).then_inc(dn_ge, 1)
                act.wait_ge(dn_ge, 4 * L + 1)
                act.activation(GL[:, 5], GL[:, 2], ACT.Ln, bias=ONES[:, 0:1]).then_inc(dn_ge, 1)
                act.activation(DZ[:, 0:4, :], DZ[:, 0:4, :], ACT.Silu).then_inc(dn_ge, 1)
                act.wait_ge(dn_gc, 2 * L + 2)
                for k in range(3):
                    a = act.activation(GT[:, 3 + k], GT[:, k], ACT.Exp)
                a.then_inc(dn_ge, 1)
                def begin(h):
                    o = 4 * L + h
                    act.wait_ge(dn_dg, o + 1)
                    act.activation(DT[:], DT[:], ACT.Exp).then_inc(dn_dt, 1)
                    act.activation(E1S[h % 2][:].rearrange("p d c n -> p d (c n)"), ACC[:, 0:2, :], ACT.Exp).then_inc(dn_e1, 1)
                    act.wait_ge(dn_tok, o + 1)
                    act.activation(KV[:].rearrange("p d c n -> p d (c n)"), MIX[:, 0:2, :], ACT.Copy).then_inc(dn_kv, 1)

                begin(0)
                for h in range(4):
                    o = 4 * L + h
                    for l in range(1, 7):
                        for d in range(2):
                            act.wait_ge(dn_y, 14 * o + 2 * l + d + 1)
                            if l > 1:
                                act.wait_ge(dn_t, 12 * o + 2 * (l - 2) + d + 1)
                            act.activation(YS[:, d].rearrange("p c n -> p (c n)"), ACC[:, d, :], ACT.Copy).then_inc(dn_yc, 1)
                    act.wait_ge(dn_uw, o + 1)
                    act.activation(WT[:].rearrange("p d c n -> p d (c n)"), ACC[:, 2:4, :], ACT.Copy).then_inc(dn_wt, 1)
                    if h < 3:
                        begin(h + 1)
                for h in range(4):
                    act.wait_ge(dn_oc, 4 * L + h + 1)
                    if h >= 2:
                        act.wait_ge(dn_ssq, 12 * L + 8 + h - 1)
                    act.activation(SQ[:, h % 2, :], DQ[:, 8 + h, :], ACT.Square).then_inc(dn_sq, 1)
                act.wait_ge(dn_var, 2 * L + 2)
                act.activation(WO[:, 1, :], WO[:, 0, :], ACT.Sqrt).then_inc(dn_root, 1)
                hi_chunks(st.h0, range(4))

            def act_net(st):
                act.wait_ge(hy_arg, 3 * st.layer + st.step + 1)
                act.activation(HD[:, 1:] if st.step == 2 else T[0:64, 1, :], T[0:64, 0, :], ACT.Sin).then_inc(hy_sin, 1)

            def act_hyena(st):
                L = st.layer
                for o in range(2):
                    n = 2 * L + o
                    for k in range(2):
                        for fc, bank in ((0, ACC), (1, MIX)):
                            act.wait_ge(hy_sp, 4 * n + 2 * k + fc + 1)
                            if 4 * n + 2 * k + fc > 0:
                                act.wait_ge(hy_spd, 4 * n + 2 * k + fc)
                            act.activation(T[:], bank[:, 1:4:2, :], ACT.Copy).then_inc(hy_odd, 1)
                        if k == 0:
                            act.wait_ge(hy_zt, n + 1)
                            act.activation(ZT, ACC[:], ACT.Copy).then_inc(hy_ztc, 1)

            def act_rope(st):
                act.wait_ge(angle_ready, 1)
                act.activation(SIN[:], ANG[:, 2, :], ACT.Sin)
                act.activation(COS[:], ANG[:, 3, :], ACT.Sin).then_inc(rope_tables, 1)

            def act_mla(st):
                act.wait_ge(rope_done, 1)
                act.activation(KM[64:96, :, :], SQ[0:32, 0, :].unsqueeze(1).to_broadcast([32, 8, S]), ACT.Copy).then_inc(kr_spread, 1)
                for h in range(8):
                    act.wait_ge(ma_max, h + 1)
                    if h:
                        act.wait_ge(ma_turned, h)
                        copy_causal(st, h - 1)
                    else:
                        act.wait_ge(rope_done, 3)
                    for tc in range(TC):
                        a = act.activation(MP[:, tc, 0:P * (tc + 1)], ACC[:, tc, 0:P * (tc + 1)], ACT.Exp, bias=MS[:, 0, tc:tc + 1],
                                           scale=96.0 ** -0.5, accum_out=MS[:, 1, tc:tc + 1])
                    a.then_inc(ma_exp, 1)
                    if h >= 2 and h % 2 == 0:
                        hi_chunks(st.h0 + h // 2 - 1, [4 + h // 2 - 1])
                act.wait_ge(ma_turned, 8)
                copy_causal(st, 7)
                hi_chunks(st.h0 + 3, [7])

            def copy_causal(st, h):
                if h >= 2:
                    act.wait_ge(ma_out, h - 1)
                act.activation(MPT[:, 1280 * (h % 2):1280 * (h % 2) + 1280],
                               MIX[:, 0:3, :].rearrange("p a b -> p (a b)")[:, 0:1280], ACT.Copy).then_inc(ma_copied, 1)

            def act_mlstm(st):
                act.wait_ge(ml_abs, 1)
                act.activation(LT[:, 1, :], LT[:, 0, :], ACT.Exp, scale=-1.0).then_inc(act_step, 1)
                act.wait_ge(act_step, 1)
                act.activation(LT[:, 2, :], LT[:, 1, :], ACT.Ln, bias=ONES[:, 0:1]).then_inc(ml_log, 1)
                act.activation(OZ[:, 8:12, :], OZ[:, 8:12, :], ACT.Sigmoid).then_inc(ml_sig, 1)
                act.wait_ge(ml_mcol, 1)
                act.activation(LN[:, 0, :], MIX[:, 0, 0:16], ACT.Exp).then_inc(ml_em, 1)
                for h in range(4):
                    act.wait_ge(ml_bcast, h + 1)
                    if h:
                        act.wait_ge(ml_sw, h)
                    for kc in range(TC):
                        a, n = COFF[kc], S - kc * P
                        d = act.activation(LE[:, a:a + P], MIX[:, 1, kc * P:kc * P + P], ACT.Exp, bias=LA[:, kc, h:h + 1])
                        if n > P:
                            act.activation(LE[:, a + P:a + n], MIX[:, 0, (kc + 1) * P:S], ACT.Exp, bias=LA[:, kc, h:h + 1])
                    d.then_inc(ml_decay, 1)
                    if h:
                        square_head(h - 1)
                square_head(3)
                act.wait_ge(ml_var, 1)
                act.activation(LN[:, 3, :], LN[:, 2, :], ACT.Sqrt).then_inc(ml_root, 1)
                hi_chunks(st.h0, range(4))

            def square_head(h):
                act.wait_ge(ml_u, h + 1)
                if h >= 2:
                    act.wait_ge(ml_ssq, h - 1)
                act.activation(SQ[:, h % 2, :], LU[:, h, :], ACT.Square).then_inc(ml_usq, 1)

            act.wait_ge(ones_ready, 2)
            split_hi(0, 0, 0)
            for st in stages:
                {"linear": act_linear, "norm": act_norm, "rms": act_rms, "mem": act_mem,
                 "even": act_even, "xattn": act_xattn, "rope": act_rope, "mla": act_mla, "mlstm": act_mlstm,
                 "net": act_net, "silu_qk": act_silu_qk, "delta": act_delta, "hyena": act_hyena}[st.kind](st)

        @block.vector
        def _(v):
            step = Steps(v, dve_step)

            def split_lo(n, add, i):
                v.wait_ge(w_hi, n + add + 1)
                v.tensor_tensor(WL[n % 2][:], RAW[n % 2][:], WH[n % 2][:], ALU.subtract).then_inc(w_lo, 1)

            def dve_linear(st):
                per = {"ffn": 2, "even": 7, "conv5": 14, "conv3": 6}.get(st.out, 0)
                n0 = step.n + st.opens
                scale = RS_OD if st.name[:3] == "od_" else RS[:]
                scale2 = scale.unsqueeze(1).to_broadcast([P, 2, S])
                if st.name == "od_in":
                    v.wait_ge(rope_tables, 1)

                def period(i):
                    if not (st.opens and isinstance(i, int) and i == 0):
                        step.n = i * per + n0
                    for j in in_period(st, i):
                        b = i * (2 * st.bpu) + (st.b0 + j)
                        pair = (st.b0 + j) % 2
                        for q in range(st.upb):
                            if st.bpu == 1 or j % st.bpu == 0:
                                n, add = unit_of(st, i, j * st.upb + q if st.bpu == 1 else j // st.bpu)
                                if st.opens and isinstance(i, int) and i == j == 0:
                                    continue
                                if not (st.last and isinstance(i, int) and n + add + 1 >= n_units):
                                    split_lo(n + 1, add, i)
                        v.wait_ge(unit_done, done_after(st, i, j))
                        if st.opens and isinstance(i, int) and i == j == 0:
                            v.wait_ge(scale_ready, st.norm.nrm + 1)
                            step(v.tensor_copy(scale, MIX[:, 1, :]))
                        two = ACC[:, 2 * pair:2 * pair + 2, :]
                        off = i * (2 * st.bpu) + j
                        if st.out in ("conv5", "conv3"):
                            taps = (0, 1, 3, 4) if st.out == "conv5" else (0, 2)
                            mid = 2 if st.out == "conv5" else 1
                            cv = i * 2 + (12 * st.layer + (6 if st.out == "conv3" else 0) + j + 1)
                            v.tensor_tensor(CVT[:, j], two, scale2, ALU.mult).then_inc(block_done, 1)
                            v.wait_ge(cv_center, cv)
                            for k in taps:
                                for m in range(2):
                                    ch = i * 4 + (2 * j + m)
                                    sh = k - mid
                                    to = slice(max(0, -sh), S - max(0, sh))
                                    fr = slice(max(0, sh), S - max(0, -sh))
                                    w = PAR2[:, bass.ds(ch + (pcol[f"{st.out}{st.layer}"][0] + 12 * k), 1)]
                                    dst = DEST[st.dest][:, bass.ds(ch, 1), to].rearrange("p a n -> p (a n)")
                                    tap = v.scalar_tensor_tensor(dst, CVT[:, j, m, fr], w, dst, ALU.mult, ALU.add)
                                    if k == taps[-1] and m == 1:
                                        tap.then_inc(cv_done, 1)
                                    else:
                                        step(tap)
                            v.wait_ge(cv_done, cv)
                        elif st.out == "fm" and st.half and isinstance(off, int) and off == st.nb - 1:
                            v.tensor_tensor(DEST[st.dest][:, 2 * off, :], two[:, 0, :], scale, ALU.mult).then_inc(block_done, 1)
                        elif st.out == "fm" and st.scaled:
                            v.tensor_tensor(DEST[st.dest][:, bass.ds(off * 2, 2), :], two, scale2, ALU.mult).then_inc(block_done, 1)
                        elif st.out == "fm":
                            v.tensor_copy(DEST[st.dest][:, bass.ds(off * 2, 2), :], two).then_inc(block_done, 1)
                        elif st.out == "fm_mem":
                            v.tensor_copy(XK[:, bass.ds(off * 2, 2), :], two[:, :, 0:M_MEM]).then_inc(block_done, 1)
                        elif st.out == "tm_mem":
                            v.tensor_copy(XV[:, :, bass.ds(off * 256, 256)],
                                          ACC[:, 2 * pair, :].rearrange("p (b n) -> p b n", b=2)).then_inc(block_done, 1)
                        elif st.out == "tm" and st.scaled:
                            v.tensor_tensor(DEST[st.dest][:, :, bass.ds(off * 256, 256)],
                                            two.rearrange("p a (b n) -> p (a b) n", b=2),
                                            RN[:, 4, :].unsqueeze(2).to_broadcast([P, TC, 256]), ALU.mult).then_inc(block_done, 1)
                        elif st.out == "tm":
                            v.tensor_copy(DEST[st.dest][:, :, bass.ds(off * 256, 256)],
                                          two.rearrange("p a (b n) -> p (a b) n", b=2)).then_inc(block_done, 1)
                        elif st.out == "nope":
                            dst = DEST[st.dest][0:64, 4 * off:4 * off + 4, :].rearrange("p (m e) n -> p m e n", e=2)
                            v.tensor_copy(dst[:, :, 0, :], two[0:64])
                            v.tensor_copy(dst[:, :, 1, :], two[64:128]).then_inc(block_done, 1)
                        elif st.out == "resid":
                            x2 = X[:, bass.ds(off * 2, 2), :]
                            v.scalar_tensor_tensor(x2, two, st.scale, x2, ALU.mult, ALU.add).then_inc(block_done, 1)
                            if st.feeds and st.feeds.early and off < st.nb - 1:
                                v.wait_ge(block_done, b + 1)
                                v.wait_ge(hid_ready, st.hidin + KF)
                                late_chunks(st.feeds, 2 * off, 2 * off + 2)
                        elif st.out == "ffn":
                            f = i * 2 + (st.ffn * KF + j)
                            v.tensor_tensor(SG[:], two[:, 0, :], scale, ALU.mult).then_inc(gate_ready, 1)
                            if not (isinstance(i, int) and f < 2):
                                v.wait_ge(hid_ready, f - 1)
                            v.tensor_tensor(T[:, j, :], two[:, 1, :], scale, ALU.mult).then_inc(block_done, 1)
                            v.wait_ge(block_done, b + 1)
                            v.wait_ge(silu_ready, f + 1)
                            step(v.tensor_tensor(T[:, j, :], T[:, j, :], SG[:], ALU.mult))
                            v.tensor_copy(HIDH[:, bass.ds(off, 1), :], T[:, j:j + 1, :]).then_inc(hid_hi, 1)
                            v.wait_ge(hid_hi, f + 1)
                            v.tensor_tensor(HIDL[:, bass.ds(off, 1), :], T[:, j:j + 1, :], HIDH[:, bass.ds(off, 1), :],
                                            ALU.subtract).then_inc(hid_ready, 1)
                        elif st.out == "even" and j == 0:
                            v.wait_ge(ev_gc, i + 1)
                            v.tensor_tensor(EV_U[:], two[:, 1, :], scale, ALU.mult).then_inc(block_done, 1)
                            v.wait_ge(block_done, b + 1)
                            step(v.tensor_tensor(EV_U[:], EV_U[:], EV_GC[:], ALU.mult))
                            step(v.tensor_tensor(EV_U[:], EV_U[:], scale, ALU.mult))
                            w = [PAR[:, bass.ds(i + (pcol["ev_conv"][0] + 4 * t), 1)] for t in range(3)]
                            step(v.tensor_scalar(EV_CV[:], EV_U[:], w[2], None, ALU.mult))
                            step(v.scalar_tensor_tensor(EV_CV[:, 1:S], EV_U[:, 0:S - 1], w[1], EV_CV[:, 1:S], ALU.mult, ALU.add))
                            step(v.scalar_tensor_tensor(EV_CV[:, 2:S], EV_U[:, 0:S - 2], w[0], EV_CV[:, 2:S], ALU.mult, ALU.add))
                        elif st.out == "even":
                            ya, one = EV_YA[:, bass.ds(i, 1), :], scale.unsqueeze(1)
                            step(v.tensor_tensor(ya, two[:, 0:1, :], one, ALU.mult))
                            step(v.tensor_tensor(ya, ya, EV_CV[:].unsqueeze(1), ALU.mult))
                            v.tensor_tensor(EV_XB[:, bass.ds(i, 1), :], two[:, 1:2, :], one, ALU.mult).then_inc(block_done, 1)
                periods(v, st, period)
                step.n = n0 + per * -(-st.nb // (2 * st.bpu))

            def chunks(h0, n, produce, dests, width=S):
                for c in range(n + 1):
                    if c < n and h0 + c >= 2:
                        v.wait_ge(h_ready, h0 + c - 1)
                    if c < n:
                        produce(c, T[:, (h0 + c) % 2, 0:width]).then_inc(t_ready, 1)
                    if c:
                        v.wait_ge(h_hi, h0 + c)
                        v.tensor_tensor(HL[:, dests[c - 1], 0:width], T[:, (h0 + c - 1) % 2, 0:width],
                                        HH[:, dests[c - 1], 0:width], ALU.subtract).then_inc(h_ready, 1)

            def inverse_root(total, root, n, count):
                step(v.reciprocal(RN[:, 1, 0:n], root))
                step(v.tensor_scalar(RN[:, 2, 0:n], total, 1.0 / count, EPS, ALU.mult, ALU.add))
                step(v.tensor_tensor(RN[:, 3, 0:n], RN[:, 1, 0:n], RN[:, 1, 0:n], ALU.mult))
                step(v.tensor_tensor(RN[:, 3, 0:n], RN[:, 3, 0:n], RN[:, 2, 0:n], ALU.mult))
                step(v.tensor_scalar(RN[:, 3, 0:n], RN[:, 3, 0:n], -0.5, 1.5, ALU.mult, ALU.add))
                step(v.tensor_tensor(RN[:, 4, 0:n], RN[:, 3, 0:n], RN[:, 1, 0:n], ALU.mult))

            def dve_diag(st):
                v.wait_ge(root_ready, st.nrm + 1)
                inverse_root(MIX[:, 0, 0:TC], RN[:, 0, :], TC, P * st.n)
                h = st.h0 + (st.n if st.late else 0)
                if h:
                    v.wait_ge(h_ready, h)
                v.tensor_tensor(DIAG.rearrange("p (a b) -> p a b", a=TC), ident4,
                                RN[:, 4, :].unsqueeze(2).to_broadcast([P, TC, P]), ALU.mult).then_inc(diag_ready, 1)

            def dve_scale(st):
                dve_diag(st)
                v.wait_ge(scale_ready, st.nrm + 1)

            def late_chunks(st, first, end):
                for c in range(first, end + 1):
                    if c < end:
                        if st.h0 + c >= 2:
                            v.wait_ge(h_ready, st.h0 + c - 1)
                        v.tensor_scalar(T[:, (st.h0 + c) % 2, :], X[:, c, :], par(st.gain, c), None, ALU.mult).then_inc(t_ready, 1)
                    if c > first:
                        v.wait_ge(h_hi, st.h0 + c)
                        v.tensor_tensor(HL[:, c - 1, :], T[:, (st.h0 + c - 1) % 2, :], HH[:, c - 1, :], ALU.subtract).then_inc(h_ready, 1)

            def dve_norm(st):
                if st.late:
                    if st.b0 == 0:
                        v.wait_ge(x_landed, 16)
                    else:
                        v.wait_ge(block_done, st.b0)
                        if st.ffn:
                            v.wait_ge(hid_ready, KF * st.ffn)
                    late_chunks(st, st.early, st.n)
                    split_lo(st.u0 + 1, 0, 0)
                    dve_diag(st)
                    return
                dve_scale(st)

                src = {"X": X, "Z": OZ, "HY": HY}[st.src]

                def produce(c, dst):
                    return v.scalar_tensor_tensor(dst, src[:, st.c0 + c, :], par(st.gain, c), MIX[:, 1, :], ALU.mult, ALU.mult)
                chunks(st.h0, st.n, produce, range(st.d0, st.d0 + st.n))
                v.tensor_copy(RN[:, 5, 0:1], EPSC[:]).then_inc(norm_done, 1)

            def dve_rms(st):
                dve_scale(st)
                if st.gain == "final":
                    v.wait_ge(par2_landed, 32)
                for c in range(KD):
                    step(v.scalar_tensor_tensor(X[:, c, :], X[:, c, :], par(st.gain, c), MIX[:, 1, :], ALU.mult, ALU.mult))
                v.tensor_copy(RN[:, 5, 0:1], EPSC[:]).then_inc(norm_done, 1)

            def dve_even(st):
                v.wait_ge(block_done, st.b0)
                cnt0 = ccol["invcnt"][0]
                for g in range(4):
                    w = 2 << g
                    src = EV_XB[:, g, :]
                    for d in range(g + 1):
                        sh = 1 << d
                        dst = EV_S[:, d % 2, :]
                        step(v.tensor_copy(dst[:, 0:sh], src[:, 0:sh]))
                        step(v.tensor_tensor(dst[:, sh:S], src[:, sh:S], src[:, 0:S - sh], ALU.add))
                        src = dst
                    step(v.scalar_tensor_tensor(EV_PD[:, g, 16:S], src[:, 16:S], 1.0 / w, EV_XB[:, g, 16:S],
                                                ALU.mult, ALU.subtract))
                    step(v.tensor_tensor(EV_PD[:, g, 0:16], src[:, 0:16], CON[:, cnt0 + 16 * g:cnt0 + 16 * g + 16], ALU.mult))
                    v.tensor_tensor(EV_PD[:, g, 0:16], EV_PD[:, g, 0:16], EV_XB[:, g, 0:16], ALU.subtract).then_inc(pooled, 1)

                def produce(c, dst):
                    if c < 4:
                        return v.tensor_copy(dst, EV_YA[:, c, :])
                    v.wait_ge(pool_ready, c - 3)
                    return v.tensor_scalar(dst, MIX[:, c - 4, :], par("pool_scale", c - 4), None, ALU.mult)
                chunks(st.h0, 8, produce, range(8))

            def dve_mem(st):
                if st.nth == 0:
                    v.wait_ge(mem_root, 1)
                    v.wait_ge(h_ready, st.h0)
                    inverse_root(MIX[:, 0, 0:MC], RN[:, 0, 0:MC], MC, D)
                    v.tensor_tensor(DIAG[:, 0:M_MEM].rearrange("p (a b) -> p a b", a=MC), ident4[:, 0:MC],
                                    RN[:, 4, 0:MC].unsqueeze(2).to_broadcast([P, MC, P]), ALU.mult).then_inc(mem_diag, 1)
                    v.wait_ge(mem_scale, 1)
                    for c in range(KD):
                        step(v.tensor_tensor(MEM[:, c, :], MEM[:, c, :], MIX[:, 1, 0:M_MEM], ALU.mult))

                def produce(c, dst):
                    return v.tensor_scalar(dst, MEM[:, c, :], par(st.gain, c), None, ALU.mult)
                chunks(st.h0, KD, produce, range(KD), M_MEM)

            def dve_xattn(st):
                o = st.nth * XH

                def maximum(h):
                    v.wait_ge(xs_scores, o + h + 1)
                    src = ACC[:, 2 * (h % 2):2 * (h % 2) + 2, :].rearrange("p a (b n) -> p (a b) n", b=2)
                    step(v.tensor_reduce(XS[:, h % 2, 2, :], src, AX.X, ALU.max))
                    v.tensor_scalar(XS[:, h % 2, 0, :], XS[:, h % 2, 2, :], -float(P) ** -0.5, None, ALU.mult)\
                        .then_inc(xs_max, 1)

                def probs(h):
                    v.wait_ge(xs_exp, o + h + 1)
                    step(v.reciprocal(XS[:, h % 2, 2, :], XS[:, h % 2, 1, :]))
                    v.tensor_tensor(XP[:, h % 2], XP[:, h % 2], XS[:, h % 2, 2, :].unsqueeze(2).to_broadcast([P, TC, M_MEM]),
                                    ALU.mult).then_inc(xs_probs, 1)

                def produce(c, dst):
                    v.wait_ge(xs_out, o + c + 1)
                    v.wait_ge(h_ready, st.h0 + c - 1)
                    return v.tensor_copy(dst, MIX[:, 2 + c % 2, :])

                def lo(c):
                    v.wait_ge(h_hi, st.h0 + c + 1)
                    v.tensor_tensor(HL[:, c, :], T[:, (st.h0 + c) % 2, :], HH[:, c, :], ALU.subtract).then_inc(h_ready, 1)

                maximum(0)
                for h in range(XH):
                    if h + 1 < XH:
                        maximum(h + 1)
                    probs(h)
                    if h >= 2:
                        produce(h - 2, T[:, (st.h0 + h - 2) % 2, :]).then_inc(t_ready, 1)
                        lo(h - 2)
                for c in (XH - 2, XH - 1):
                    produce(c, T[:, (st.h0 + c) % 2, :]).then_inc(t_ready, 1)
                    lo(c)

            def dve_rope(st):
                v.wait_ge(pos_landed, 16)
                step(v.tensor_copy(ANG[:, 0, :], POSI[:]))
                step(v.tensor_scalar(ANG[:, 0, :], ANG[:, 0, :], freq, None, ALU.mult))
                for dst, quarter in ((2, 0.0), (3, 0.25)):
                    step(v.tensor_scalar(ANG[:, 1, :], ANG[:, 0, :], TURN, quarter, ALU.mult, ALU.add))
                    step(v.tensor_scalar(ANG[:, 1, :], ANG[:, 1, :], ROUND, None, ALU.add))
                    step(v.tensor_scalar(ANG[:, 1, :], ANG[:, 1, :], ROUND, None, ALU.subtract))
                    step(v.scalar_tensor_tensor(ANG[:, dst, :], ANG[:, 1, :], -PI2[0], ANG[:, 0, :], ALU.mult, ALU.add))
                    step(v.scalar_tensor_tensor(ANG[:, dst, :], ANG[:, 1, :], -PI2[1], ANG[:, dst, :], ALU.mult, ALU.add))
                    step(v.scalar_tensor_tensor(ANG[:, dst, :], ANG[:, 1, :], -PI2[2], ANG[:, dst, :], ALU.mult, ALU.add))
                    step(v.tensor_scalar(ANG[:, dst, :], ANG[:, dst, :], quarter * 2 * np.pi, PI_IN, ALU.add, ALU.min))
                    step(v.tensor_scalar(ANG[:, dst, :], ANG[:, dst, :], -PI_IN, None, ALU.max))
                v.tensor_copy(RN[:, 5, 0:1], EPSC[:]).then_inc(angle_ready, 1)

            def dve_mla(st):
                v.wait_ge(rope_tables, 1)
                v.wait_ge(rotated, 3)
                step(v.tensor_tensor(T[0:32, 0, :], OZ[0:32, 17, :], COS[0:32, :], ALU.mult))
                step(v.tensor_tensor(T[0:32, 1, :], MIX[0:32, 2, :], SIN[0:32, :], ALU.mult))
                v.tensor_tensor(SQ[0:32, 0, :], T[0:32, 0, :], T[0:32, 1, :], ALU.add).then_inc(rope_done, 1)
                v.wait_ge(rope_done, 1)
                for m in range(2):
                    step(v.tensor_tensor(T[:, 0, :], QR[:, m, :], COS[:], ALU.mult))
                    step(v.tensor_tensor(T[:, 1, :], MIX[:, m, :], SIN[:], ALU.mult))
                    for j in range(4):
                        r = slice(32 * j, 32 * j + 32)
                        a = v.tensor_tensor(QM[64:96, 4 * m + j, :], T[r, 0, :], T[r, 1, :], ALU.add)
                    a.then_inc(rope_done, 1)
                    v.wait_ge(rope_done, m + 2)

                def maximum(h):
                    v.wait_ge(ma_scores, h + 1)
                    for tc in range(TC):
                        step(v.tensor_reduce(MS[:, 2, tc:tc + 1], ACC[:, tc, 0:P * (tc + 1)], AX.X, ALU.max))
                    v.tensor_scalar(MS[:, 0, :], MS[:, 2, :], -96.0 ** -0.5, None, ALU.mult).then_inc(ma_max, 1)

                def probs(h):
                    v.wait_ge(ma_exp, h + 1)
                    step(v.reciprocal(MS[:, 2, :], MS[:, 1, :]))
                    for tc in range(TC):
                        a = v.tensor_scalar(MP[:, tc, 0:P * (tc + 1)], MP[:, tc, 0:P * (tc + 1)], MS[:, 2, tc:tc + 1], None, ALU.mult)
                    a.then_inc(ma_probs, 1)
                    v.wait_ge(ma_probs, h + 1)

                def pair(c):
                    v.wait_ge(ma_out, 2 * c + 2)
                    v.wait_ge(h_ready, st.h0 + c - 1)
                    v.tensor_copy(T[:, (st.h0 + c) % 2, :], MIX[:, 3, :]).then_inc(t_ready, 1)
                    v.wait_ge(h_hi, st.h0 + c + 1)
                    v.tensor_tensor(HL[:, 4 + c, :], T[:, (st.h0 + c) % 2, :], HH[:, 4 + c, :], ALU.subtract).then_inc(h_ready, 1)

                maximum(0)
                for h in range(8):
                    probs(h)
                    if h < 7:
                        maximum(h + 1)
                    if h >= 2 and h % 2 == 0:
                        pair(h // 2 - 1)
                pair(3)

            def dve_mlstm(st):
                bias = PAR[:, pcol["gbias"][0]:pcol["gbias"][0] + 8]
                LGf = LG[:].rearrange("p a b -> p (a b)")
                v.wait_ge(ml_turned, 1)
                step(v.tensor_tensor(LG[:], MIX[:, 0, 0:32].rearrange("p (a b) -> p a b", a=TC),
                                     bias.unsqueeze(1).to_broadcast([P, TC, 8]), ALU.add))
                f, i = LG[:, :, 4:8], LG[:, :, 0:4]
                v4 = lambda ap: ap.rearrange("p (a b) -> p a b", a=TC)
                v.scalar_tensor_tensor(v4(LT[:, 0, :]), f, -1.0, f, ALU.mult, ALU.max).then_inc(ml_abs, 1)
                v.wait_ge(ml_log, 1)
                v.scalar_tensor_tensor(LL[:], f, 0.0, v4(LT[:, 2, :]), ALU.min, ALU.subtract).then_inc(ml_ls, 1)
                v.wait_ge(ml_f, 1)
                F = v4(MIX[:, 1, 0:16])
                v.tensor_tensor(LA[:], i, F, ALU.subtract)
                v.tensor_copy(LF[:], F).then_inc(ml_af, 1)
                v.wait_ge(ml_rows, 1)
                step(v.tensor_copy(LR[:, 0:2, :], MIX[0:4, 2:4, :]))
                step(v.tensor_tensor_scan(LR[:, 2, :], LR[:, 0, :], LR[:, 0, :], 0.0, ALU.max, ALU.max))
                step(v.scalar_tensor_tensor(LR[:, 3, :], LR[:, 1, :], -1.0, LR[:, 2, :], ALU.mult, ALU.subtract))
                v.tensor_scalar(LR[:, 2, :], LR[:, 2, :], -1.0, None, ALU.mult).then_inc(ml_rowsm, 1)
                v.wait_ge(ml_rowsm, 1)
                v.wait_ge(ml_em, 1)
                v.wait_ge(ml_sig, 1)
                for h in range(4):
                    v.wait_ge(ml_scores, h + 1)
                    v.wait_ge(ml_decay, h + 1)
                    if h >= 2:
                        v.wait_ge(ml_num, h - 1)
                    v.scalar_tensor_tensor(LW[:, h % 2, :], ACC[:].rearrange("p a b -> p (a b)")[:, 0:1280], float(P) ** -0.5,
                                           LE[:], ALU.mult, ALU.mult).then_inc(ml_sw, 1)
                    v.wait_ge(ml_num, h + 1)
                    v.tensor_tensor(LU[:, h, :], MIX[:, 3, :], OZ[:, 8 + h, :], ALU.mult).then_inc(ml_u, 1)
                v.wait_ge(ml_ssq, 4)
                step(v.tensor_copy(LN[:, 1, :], MIX[:, 2, 0:16]))
                step(v.scalar_tensor_tensor(LN[:, 1, :], LN[:, 1, :], -1.0, LN[:, 1, :], ALU.mult, ALU.max))
                step(v.tensor_tensor(LN[:, 1, :], LN[:, 1, :], LN[:, 0, :], ALU.max))
                step(v.reciprocal(LN[:, 4, :], LN[:, 1, :]))
                step(v.tensor_tensor(LN[:, 5, :], LN[:, 4, :], LN[:, 4, :], ALU.mult))
                step(v.tensor_tensor(LN[:, 5, :], LN[:, 5, :], MIX[:, 2, 16:32], ALU.mult))
                v.tensor_scalar(LN[:, 2, :], LN[:, 5, :], 1.0 / P, EPS, ALU.mult, ALU.add).then_inc(ml_var, 1)
                v.wait_ge(ml_root, 1)
                newton(LN[:, 6, :], LN[:, 2, :], LN[:, 3, :], LN[:, 7, :], LN[:, 5, :])
                step(v.tensor_tensor(LN[:, 6, :], LN[:, 6, :], LN[:, 4, :], ALU.mult))
                for h in range(4):
                    if h >= 2:
                        v.wait_ge(ml_scale, h - 1)
                    col = v4(LN[:, 6, :])[:, :, h:h + 1]
                    v.tensor_tensor(LE[:, 512 * (h % 2):512 * (h % 2) + 512].rearrange("p (a b) -> p a b", a=TC), ident4,
                                    col.to_broadcast([P, TC, P]), ALU.mult).then_inc(ml_diag, 1)
                    if h:
                        out_head(st, h - 1)
                out_head(st, 3)

            def out_head(st, h):
                v.wait_ge(ml_scale, h + 1)
                v.wait_ge(h_ready, st.h0 + h - 1)
                v.scalar_tensor_tensor(T[:, (st.h0 + h) % 2, :], LU[:, h, :], par("mln", h), MIX[:, h % 2, :], ALU.mult, ALU.mult)\
                    .then_inc(t_ready, 1)
                v.wait_ge(h_hi, st.h0 + h + 1)
                v.tensor_tensor(HL[:, h, :], T[:, (st.h0 + h) % 2, :], HH[:, h, :], ALU.subtract).then_inc(h_ready, 1)

            def dve_delta(st):
                L = st.layer
                v.wait_ge(silu_done, 2 * L + 1)
                v.wait_ge(dn_ssq, 12 * L + 8)
                v.tensor_scalar(RQ[:, 0, :], MIX[:, 2, 0:32], 1e-6, None, ALU.add).then_inc(dn_var, 1)
                v.wait_ge(dn_root, 2 * L + 1)
                newton(RQ[:, 4, :], RQ[:, 0, :], RQ[:, 1, :], RQ[:, 2, :], RQ[:, 3, :])
                v.wait_ge(dn_g16, L + 1)
                step(v.tensor_copy(G16[:], MIX[:, 3, 0:64].rearrange("p (c g) -> p c g", c=TC)))
                dtb = PAR2[:, pcol[f"dtb{L}"][0]:pcol[f"dtb{L}"][0] + 8].unsqueeze(1).to_broadcast([P, TC, 8])
                step(v.tensor_tensor(G16[:, :, 8:16], G16[:, :, 8:16], dtb, ALU.add))
                al = G16[:, :, 8:16]
                v.scalar_tensor_tensor(GL[:, 1], al, -1.0, al, ALU.mult, ALU.max).then_inc(dn_gv, 1)
                v.wait_ge(h_ready, st.h0)
                for h in range(4):
                    if h >= 2:
                        v.wait_ge(dn_scale, 8 * L + h - 1)
                    v.tensor_tensor(T[:, h % 2, :].rearrange("p (a b) -> p a b", a=TC), ident4,
                                    RQ[:, 4, 16 + 4 * h:20 + 4 * h].unsqueeze(2).to_broadcast([P, TC, P]), ALU.mult)\
                        .then_inc(dn_diag, 1)
                    if h:
                        v.wait_ge(dn_scale, 8 * L + h)
                        v.tensor_tensor(DQ[:, 3 + h, :], DQ[:, 3 + h, :], MIX[:, (h - 1) % 2, :], ALU.mult).then_inc(dn_kn, 1)
                v.wait_ge(dn_scale, 8 * L + 4)
                v.tensor_tensor(DQ[:, 7, :], DQ[:, 7, :], MIX[:, 1, :], ALU.mult).then_inc(dn_kn, 1)
                v.wait_ge(dn_ge, 4 * L + 2)
                step(v.scalar_tensor_tensor(GL[:, 3], al, 0.0, GL[:, 5], ALU.max, ALU.add))
                v.scalar_tensor_tensor(GL[:, 3], GL[:, 3], -1.0, GL[:, 4, 0, :].unsqueeze(1).to_broadcast([P, TC, 8]),
                                       ALU.mult, ALU.mult).then_inc(dn_gv, 1)
                v.wait_ge(dn_gc, 2 * L + 1)
                dch = lambda ap: ap.rearrange("p c (d h) -> p d c h", d=2)
                gsum = dch(MIX[:, 3, 96:128].rearrange("p (c g) -> p c g", c=TC))
                flat = lambda ap: ap.rearrange("p d c h -> p (d c h)")
                for d in range(2):
                    step(v.tensor_copy(GT[:, 0, d], MIX[:, 3, 64 + 16 * d:80 + 16 * d].rearrange("p (c h) -> p c h", c=TC)))
                    step(v.tensor_copy(GT[:, 2, d], gsum[:, d]))
                    step(v.tensor_copy(GT[:, 6, d], dch(GL[:, 0])[:, d]))
                step(v.tensor_tensor(GT[:, 1], GT[:, 2], GT[:, 0], ALU.subtract))
                v.tensor_scalar(GT[:, 7], GT[:, 6], -1.0, None, ALU.mult).then_inc(dn_gc, 1)
                v.wait_ge(dn_gc, 2 * L + 2)
                v.wait_ge(dn_ge, 4 * L + 4)
                G, EG, ELG, EL, BETA, NBETA = GT[:, 0], GT[:, 3], GT[:, 4], GT[:, 5], GT[:, 6], GT[:, 7]
                over = lambda tab, h: tab[:, :, :, h:h + 1].to_broadcast([P, 2, TC, P])
                both = lambda ap: ap.rearrange("p d (c n) -> p d c n", c=TC)
                kq = ACC[:, 2:4, :].rearrange("p a (b s n) -> p (a b) s n", b=2, s=2)
                def differences(h):
                    v.wait_ge(dn_gb, 4 * L + h + 1)
                    if h:
                        v.wait_ge(dn_b, 7 * (4 * L + h))
                    step(v.tensor_tensor(DT[:], both(ACC[:, 0:2, :]), over(G, h), ALU.subtract))
                    v.tensor_scalar(DT[:], DT[:], 0.0, None, ALU.min).then_inc(dn_dg, 1)

                def causal(h):
                    v.wait_ge(dn_dt, 4 * L + h + 1)
                    for d, m in ((0, tri), (1, triT)):
                        step(v.tensor_tensor(DT[:, d], DT[:, d], m.unsqueeze(1).to_broadcast([P, TC, P]), ALU.mult))

                def attention(h):
                    v.wait_ge(dn_kq, 4 * L + h + 1)
                    for d in range(2):
                        step(v.tensor_tensor(ATS[h % 2][:, d], DT[:, d], kq[:, :, 0, :], ALU.mult))

                def matrix(h):
                    for d in range(2):
                        step(v.tensor_tensor(DT[:, d], DT[:, d], kq[:, :, 1, :], ALU.mult))
                    v.tensor_tensor(DT[:], DT[:], over(BETA, h), ALU.mult).then_inc(dn_at, 1)

                differences(0)
                causal(0)
                attention(0)
                matrix(0)
                for h in range(4):
                    o = 4 * L + h
                    v.wait_ge(dn_b, 7 * o + 1)
                    eye = ident.unsqueeze(1).to_broadcast([P, TC, P])
                    for d in range(2):
                        step(v.tensor_tensor(XIT[:, d], eye, BL[:, 0, d], ALU.subtract))
                        v.wait_ge(dn_y, 14 * o + d + 1)
                        v.tensor_tensor(XI[:, d], eye, MIX[:, d, :].rearrange("p (c n) -> p c n", c=TC), ALU.subtract)\
                            .then_inc(dn_x, 1)
                    v.wait_ge(dn_e1, o + 1)
                    q = DQ[:, h, :].rearrange("p (c n) -> p c n", c=TC)
                    for d in range(2):
                        step(v.tensor_tensor(E1S[h % 2][:, d], E1S[h % 2][:, d], q, ALU.mult))
                    v.wait_ge(dn_kv, o + 1)
                    k = KV[:, 0]
                    for d in range(2):
                        step(v.tensor_tensor(KG[:, d], k, EG[:, d, :, h:h + 1].to_broadcast([P, TC, P]), ALU.mult))
                        a = v.tensor_tensor(KD_[:, d], k, ELG[:, d, :, h:h + 1].to_broadcast([P, TC, P]), ALU.mult)
                        if d == 1:
                            a.then_inc(dn_kgd, 1)
                    for l in range(1, 7):
                        for d in range(2):
                            v.wait_ge(dn_t, 12 * o + 2 * (l - 1) + d + 1)
                            tb, ttb = (ACC[:, 2], ACC[:, 3]) if d == 0 else (MIX[:, 0], MIX[:, 1])
                            if l < 6:
                                step(v.tensor_tensor(XI[:, d], XI[:, d], tb.rearrange("p (c n) -> p c n", c=TC), ALU.subtract))
                            v.tensor_tensor(XIT[:, d], XIT[:, d], ttb.rearrange("p (c n) -> p c n", c=TC), ALU.subtract)\
                                .then_inc(dn_x, 1)
                            v.wait_ge(dn_x, 14 * o + 2 * l + d + 1)
                    v.wait_ge(dn_uw, o + 1)
                    v.tensor_tensor(UB[:], both(ACC[:, 0:2, :]), over(BETA, h), ALU.mult).then_inc(dn_ub, 1)
                    v.wait_ge(dn_ub, o + 1)
                    if h < 3:
                        differences(h + 1)
                    for s in range(TC):
                        at = (s, TC - 1 - s)
                        if s and h < 3:
                            (causal, attention, matrix)[s - 1](h + 1)
                        if s:
                            v.wait_ge(dn_w, 3 * o + s)
                            for d in range(2):
                                a = v.scalar_tensor_tensor(UB[:, d, at[d], :], MIX[:, 2, d * P:d * P + P], NBETA[:, d, at[d], h:h + 1],
                                                           UB[:, d, at[d], :], ALU.mult, ALU.add)
                            a.then_inc(dn_vn, 1)
                        if s < TC - 1:
                            v.wait_ge(dn_upd, 3 * o + s + 1)
                            for d in range(2):
                                up = MIX[:, 2, 256 + d * P:256 + d * P + P]
                                if s == 0:
                                    a = v.tensor_copy(ST[:, 0, d, :], up)
                                else:
                                    a = v.scalar_tensor_tensor(ST[:, s % 2, d, :], ST[:, (s - 1) % 2, d, :], EL[:, d, at[d], h:h + 1],
                                                               up, ALU.mult, ALU.add)
                            a.then_inc(dn_s, 1)
                            v.wait_ge(dn_s, 3 * o + s + 1)
                    v.wait_ge(dn_o, o + 1)
                    v.tensor_copy(DQ[:, 8 + h, :], MIX[:, 3, :]).then_inc(dn_oc, 1)
                v.wait_ge(dn_ssq, 12 * L + 12)
                step(v.tensor_scalar(WO[:, 2, :], RQ[:, 4, 0:16], float(P) ** -0.5, None, ALU.mult))
                step(v.tensor_tensor(WO[:, 3, :], WO[:, 2, :], WO[:, 2, :], ALU.mult))
                step(v.tensor_tensor(WO[:, 3, :], WO[:, 3, :], MIX[:, 2, 0:16], ALU.mult))
                v.tensor_scalar(WO[:, 0, :], WO[:, 3, :], 1.0 / P, EPS, ALU.mult, ALU.add).then_inc(dn_var, 1)
                v.wait_ge(dn_root, 2 * L + 2)
                newton(WO[:, 4, :], WO[:, 0, :], WO[:, 1, :], WO[:, 5, :], WO[:, 6, :])
                step(v.tensor_tensor(WO[:, 4, :], WO[:, 4, :], WO[:, 2, :], ALU.mult))
                for h in range(5):
                    if h < 4:
                        if h >= 2:
                            v.wait_ge(dn_scale, 8 * L + 4 + h - 1)
                        v.tensor_tensor(KV[:, h % 2], ident4, WO[:, 4, 4 * h:4 * h + 4].unsqueeze(2).to_broadcast([P, TC, P]),
                                        ALU.mult).then_inc(dn_diag, 1)
                    if h:
                        c = h - 1
                        v.wait_ge(dn_scale, 8 * L + 4 + h)
                        v.wait_ge(h_ready, st.h0 + c - 1)
                        slot = T[:, (st.h0 + c) % 2, :]
                        step(v.scalar_tensor_tensor(slot, DQ[:, 8 + c, :], par(f"dnn{L}"), MIX[:, c % 2, :], ALU.mult, ALU.mult))
                        v.tensor_tensor(slot, slot, DZ[:, c, :], ALU.mult).then_inc(t_ready, 1)
                        v.wait_ge(h_hi, st.h0 + c + 1)
                        v.tensor_tensor(HL[:, c, :], slot, HH[:, c, :], ALU.subtract).then_inc(h_ready, 1)

            def dve_net(st):
                L, i = st.layer, st.step
                p0 = pcol[f"mlp{L}"][0]
                if i == 0:
                    v.memset(HD[:, 0:1], 0.0).then_inc(hy_zero, 1)
                v.wait_ge(hy_lin, 3 * L + i + 1)
                a, b, c = SQ[0:64, 0, :], SQ[0:64, 1, :], T[0:64, 0, :]
                step(v.tensor_scalar(a, MIX[0:64, 2, :], PAR2[0:64, p0 + i:p0 + i + 1], PAR2[0:64, p0 + 3:p0 + 4], ALU.add, ALU.mult))
                step(v.tensor_scalar(b, a, TURN, ROUND, ALU.mult, ALU.add))
                step(v.tensor_scalar(b, b, ROUND, None, ALU.subtract))
                step(v.scalar_tensor_tensor(a, b, -PI2[0], a, ALU.mult, ALU.add))
                step(v.scalar_tensor_tensor(a, b, -PI2[1], a, ALU.mult, ALU.add))
                step(v.scalar_tensor_tensor(a, b, -PI2[2], a, ALU.mult, ALU.add))
                v.tensor_scalar(c, a, PI_IN, -PI_IN, ALU.min, ALU.max).then_inc(hy_arg, 1)

            def dve_hyena(st):
                L = st.layer
                def combine(n, fc, dst):
                    bank = (ACC, MIX)[fc]
                    v.wait_ge(hy_odd, n + fc + 1)
                    v.tensor_tensor(dst[:, fc, 0, :], bank[:, 0, :], T[:, 0, :], ALU.add)
                    v.tensor_tensor(dst[:, fc, 1, :], bank[:, 0, :], T[:, 0, :], ALU.subtract)
                    v.tensor_tensor(dst[:, fc, 2, :], bank[:, 2, :], T[:, 1, :], ALU.add)
                    v.tensor_tensor(dst[:, fc, 3, :], T[:, 1, :], bank[:, 2, :], ALU.subtract).then_inc(hy_spd, 1)

                def cosines(fc):
                    step(v.tensor_tensor(PT2[:, 0:2, :], ZS[:, fc, 0:2, :], KS[:, fc, 0:2, :], ALU.mult))
                    step(v.tensor_tensor(PT2[:, 2:4, :], ZS[:, fc, 2:4, :], KS[:, fc, 2:4, :], ALU.mult))
                    step(v.tensor_tensor(YT[:, 0:2, :], PT2[:, 0:2, :], PT2[:, 2:4, :], ALU.subtract))

                def sines(fc):
                    step(v.tensor_tensor(PT2[:, 0:2, :], ZS[:, fc, 0:2, :], KS[:, fc, 2:4, :], ALU.mult))
                    step(v.tensor_tensor(PT2[:, 2:4, :], ZS[:, fc, 2:4, :], KS[:, fc, 0:2, :], ALU.mult))
                    step(v.tensor_tensor(YT[:, 2:4, :], PT2[:, 0:2, :], PT2[:, 2:4, :], ALU.add))
                    v.tensor_tensor(ZS[:, fc, 0, :], YT[:, 0, :], YT[:, 1, :], ALU.add)
                    v.tensor_tensor(ZS[:, fc, 1, :], YT[:, 2, :], YT[:, 3, :], ALU.subtract)
                    v.tensor_tensor(ZS[:, fc, 2, :], YT[:, 0, :], YT[:, 1, :], ALU.subtract)
                    v.tensor_tensor(ZS[:, fc, 3, :], YT[:, 2, :], YT[:, 3, :], ALU.add).then_inc(hy_a, 1)

                for o in range(2):
                    n = 2 * L + o
                    for q in range(4):
                        v.wait_ge(hy_f, 4 * n + q + 1)
                        v.wait_ge(hy_dec[q % 2], 16 * (2 * n + q // 2 + 1))
                        a, b = SQ[:, 0, :], SQ[:, 1, :]
                        step(v.tensor_tensor(a, ACC[:, 2 * (q % 2), :], DEC[:, q % 2, 0, :], ALU.mult))
                        step(v.tensor_tensor(b, ACC[:, 2 * (q % 2) + 1, :], DEC[:, q % 2, 1, :], ALU.mult))
                        v.tensor_tensor(FS[:, 0, q, :], a, b, ALU.add)
                        v.tensor_tensor(FS[:, 1, q, :], a, b, ALU.subtract).then_inc(hy_fd, 1)
                        v.wait_ge(hy_fd, 4 * n + q + 1)
                    combine(4 * n, 0, KS)
                    combine(4 * n, 1, KS)
                    combine(4 * n + 2, 0, ZS)
                    v.wait_ge(hy_spd, 4 * n + 3)
                    cosines(0)
                    combine(4 * n + 2, 1, ZS)
                    v.wait_ge(hy_spd, 4 * n + 4)
                    sines(0)
                    v.wait_ge(hy_a, 2 * n + 1)
                    cosines(1)
                    sines(1)
                    v.wait_ge(hy_a, 2 * n + 2)
                    for m in range(4):
                        v.wait_ge(hy_y, 4 * n + m + 1)
                        y = MIX[:, m, :].rearrange("p (two t) -> p t two", two=2)
                        z = HY[:, m, :].rearrange("p (t two) -> p t two", two=2)
                        step(v.scalar_tensor_tensor(z, z, par(f"skip{L}", 4 * o + m), y, ALU.mult, ALU.add))
                        v.tensor_tensor(HY[:, m, :], HY[:, m, :], HY[:, 4 + 4 * o + m, :], ALU.mult).then_inc(hy_z, 1)

            def newton(out_ap, val, root, a, b):
                step(v.reciprocal(a, root))
                step(v.tensor_tensor(b, a, a, ALU.mult))
                step(v.tensor_tensor(b, b, val, ALU.mult))
                step(v.tensor_scalar(b, b, -0.5, 1.5, ALU.mult, ALU.add))
                step(v.tensor_tensor(out_ap, a, b, ALU.mult))

            v.memset(EPSC[:], EPS).then_inc(ones_ready, 1)
            v.memset(ONES[:], 1.0).then_inc(ones_ready, 1)
            v.wait_ge(ones_ready, 2)
            v.wait_ge(par_landed, 32)
            split_lo(0, 0, 0)
            for st in stages:
                {"linear": dve_linear, "norm": dve_norm, "rms": dve_rms, "mem": dve_mem,
                 "even": dve_even, "xattn": dve_xattn, "rope": dve_rope, "mla": dve_mla, "mlstm": dve_mlstm,
                 "net": dve_net, "silu_qk": lambda st: None, "delta": dve_delta, "hyena": dve_hyena}[st.kind](st)
            if isinstance(step.n, int) and step.n:
                v.wait_ge(dve_step, step.n)


def kernel(**inputs):
    import concourse.bacc as _bacc
    from concourse.bass_utils import run_bass_kernel_spmd as _run

    t = {k: np.asarray(v) for k, v in inputs.items()}
    stages, _ = schedule()
    arrays = {
        "wall": pack_weights(t, stages),
        "xT": np.ascontiguousarray(t["x"][0].T.reshape(KD, P, S).transpose(1, 0, 2)),
        "memT": np.ascontiguousarray(t["mem"][0].T.reshape(KD, P, M_MEM).transpose(1, 0, 2)),
        "params": pack_params(t),
        "consts": const_columns()[1],
        "pos": np.ascontiguousarray(np.broadcast_to(t["positions"][0], (P, S))),
        "poolw": np.ascontiguousarray(t["ev_pool_w"][0].transpose(1, 0, 2)),
        "params2": pack_params2(t),
        "consts2": const2_columns()[1],
        "feats": hyena_constants()[0], "decays": hyena_constants()[1], "mats": hyena_constants()[2],
        "filters": pack_filters(t),
    }
    nc = _bacc.Bacc("TRN2", target_bir_lowering=False, num_devices=1)
    args = [nc.dram_tensor(n, a.shape, mybir.dt.from_np(a.dtype), kind="ExternalInput").ap() for n, a in arrays.items()]
    args.append(nc.dram_tensor("y", (P, KD, S), F32, kind="ExternalOutput").ap())
    build(nc, *args)
    r = _run(nc, [arrays], core_ids=[0])
    y = np.asarray(r.results[0]["y"])
    return y.transpose(1, 0, 2).reshape(D, S).T.reshape(1, S, D)
```
